# Optimizing a Trainium2 kernel written in Bass

```python
import jax, jax.numpy as jnp
from jax import lax
import numpy as np

D_MODEL = 1024
BATCH = 1
SEQ = 256
DEPTH = 1

CHUNK = 64
EPS = 1e-6
GLA_HEADS = 4
GLA_DK = 128
GLA_DV = 128
GLA_LOWRANK = 16
GLA_TAU = 16.0
GLA_QK = GLA_HEADS * GLA_DK
GLA_V = GLA_HEADS * GLA_DV
SGU_GROUPS = 4
SGU_GROUP_DIM = 128
SGU_BLOCK = 128
SGU_W = SGU_GROUPS * SGU_GROUP_DIM
PEER_HEADS = 8
PEER_DKEY = 256
PEER_NKEYS = 128
PEER_TOPK = 16
PEER_EXPERTS = PEER_NKEYS * PEER_NKEYS
PEER_TOKEN_BLOCK = 128
IN_COLS = (GLA_QK, GLA_QK, GLA_V, GLA_V, GLA_LOWRANK, SGU_W, SGU_W, D_MODEL, D_MODEL)
IN_WIDTH = sum(IN_COLS)


def rmsnorm(x, g):
    xf = x.astype(jnp.float32)
    y = xf * lax.rsqrt(jnp.mean(xf * xf, axis=-1, keepdims=True) + EPS)
    return (y * g.astype(jnp.float32)).astype(x.dtype)

def gla_branch(q, k, v, r, a_lr, w_a2, b_a, g_out):
    B, S, _ = q.shape
    NC = S // CHUNK
    f32 = jnp.float32
    qc = q.astype(f32).reshape(B, NC, CHUNK, GLA_HEADS, GLA_DK) * (GLA_DK ** -0.5)
    kc = k.astype(f32).reshape(B, NC, CHUNK, GLA_HEADS, GLA_DK)
    vc = v.astype(f32).reshape(B, NC, CHUNK, GLA_HEADS, GLA_DV)
    log_a = jax.nn.log_sigmoid((a_lr @ w_a2 + b_a).astype(f32)) / GLA_TAU
    log_a = log_a.reshape(B, NC, CHUNK, GLA_HEADS, GLA_DK)
    cum = jnp.cumsum(log_a, axis=2)
    total = cum[:, :, -1]
    k_dec = kc * jnp.exp(total[:, :, None] - cum)
    chunk_kv = jnp.einsum('bnchk,bnchv->bnhkv', k_dec, vc)
    decay = jnp.exp(total)

    def step(state, inp):
        dec, kv, qq = inp
        state = dec[..., None] * state + kv
        out = jnp.einsum('bchk,bhkv->bchv', qq, state)
        return state, out

    init = jnp.zeros((B, GLA_HEADS, GLA_DK, GLA_DV), f32)
    _, o = lax.scan(step, init, (jnp.moveaxis(decay, 1, 0), jnp.moveaxis(chunk_kv, 1, 0),
                                 jnp.moveaxis(qc, 1, 0)))
    o = jnp.moveaxis(o, 0, 1).reshape(B, S, GLA_HEADS, GLA_DV)
    o = o * lax.rsqrt(jnp.mean(o * o, axis=-1, keepdims=True) + EPS)
    o = o.reshape(B, S, GLA_V) * g_out.astype(f32)
    return (o * jax.nn.silu(r.astype(f32))).astype(q.dtype)

def sgu_branch(u, v, ln_g, ln_b, w_s, b_s):
    B, S, _ = v.shape
    f32 = jnp.float32
    vf = v.astype(f32)
    mu = jnp.mean(vf, axis=-1, keepdims=True)
    var = jnp.mean(jnp.square(vf - mu), axis=-1, keepdims=True)
    vn = (vf - mu) * lax.rsqrt(var + EPS) * ln_g.astype(f32) + ln_b.astype(f32)
    NB = S // SGU_BLOCK
    vn = vn.reshape(B, NB, SGU_BLOCK, SGU_GROUPS, SGU_GROUP_DIM)
    pos = jnp.arange(SGU_BLOCK) // CHUNK
    mask = pos[:, None] >= pos[None, :]
    w = jnp.where(mask[None], w_s.astype(f32), 0.0)
    mixed = jnp.einsum('gij,bnjgc->bnigc', w, vn) + b_s.astype(f32).T[None, None, :, :, None]
    return (u.astype(f32) * mixed.reshape(B, S, SGU_W)).astype(u.dtype)

def peer(x, w_q, sub_k1, sub_k2, expert_u, expert_v):
    B, S, D = x.shape
    T = B * S
    f32 = jnp.float32
    xt = x.reshape(T, D)
    q = (xt @ w_q).astype(f32).reshape(T, PEER_HEADS, 2, PEER_DKEY // 2)
    s1 = jnp.einsum('thd,kd->thk', q[:, :, 0], sub_k1.astype(f32))
    s2 = jnp.einsum('thd,kd->thk', q[:, :, 1], sub_k2.astype(f32))
    v1, i1 = lax.top_k(s1, PEER_TOPK)
    v2, i2 = lax.top_k(s2, PEER_TOPK)
    cand = (v1[..., :, None] + v2[..., None, :]).reshape(T, PEER_HEADS, PEER_TOPK * PEER_TOPK)
    vals, ci = lax.top_k(cand, PEER_TOPK)
    ia = ci // PEER_TOPK
    ib = ci % PEER_TOPK
    idx = jnp.take_along_axis(i1, ia, axis=-1) * PEER_NKEYS + jnp.take_along_axis(i2, ib, axis=-1)
    gates = jax.nn.softmax(vals, axis=-1)
    NBLK = T // PEER_TOKEN_BLOCK
    HK = PEER_HEADS * PEER_TOPK
    idx = idx.reshape(NBLK, PEER_TOKEN_BLOCK, HK)
    gates = gates.reshape(NBLK, PEER_TOKEN_BLOCK, HK)
    xb = xt.reshape(NBLK, PEER_TOKEN_BLOCK, D)

    def block(args):
        xx, ii, gg = args
        u = expert_u[ii]
        h = jnp.einsum('tkd,td->tk', u, xx).astype(f32)
        a = (jax.nn.gelu(h) * gg).astype(x.dtype)
        return jnp.einsum('tk,tkd->td', a, expert_v[ii])

    out = lax.map(block, (xb, idx, gates))
    return out.reshape(B, S, D)

def first_inputs(seed: int = 0) -> dict:
    key = jax.random.key(seed)
    ks = jax.random.split(key, 24)
    f32 = jnp.float32
    L, D = DEPTH, D_MODEL
    nrm = lambda k, shape, scale: jax.random.normal(k, shape, f32) * scale
    return {
        "x": jax.random.normal(ks[0], (BATCH, SEQ, D), f32),
        "norm1_g": 1.0 + nrm(ks[1], (L, D), 0.02),
        "w_in": nrm(ks[2], (L, D, IN_WIDTH), D ** -0.5),
        "w_gate_up": nrm(ks[3], (L, GLA_LOWRANK, GLA_QK), GLA_LOWRANK ** -0.5),
        "b_gate": 1.0 + nrm(ks[4], (L, GLA_QK), 0.1),
        "gla_norm_g": 1.0 + nrm(ks[5], (L, GLA_V), 0.02),
        "sgu_ln_g": 1.0 + nrm(ks[6], (L, SGU_W), 0.02),
        "sgu_ln_b": nrm(ks[7], (L, SGU_W), 0.02),
        "sgu_w": nrm(ks[8], (L, SGU_GROUPS, SGU_BLOCK, SGU_BLOCK), 0.5 * SGU_BLOCK ** -0.5),
        "sgu_b": 1.0 + nrm(ks[9], (L, SGU_GROUPS, SGU_BLOCK), 0.02),
        "w_branch_a": nrm(ks[10], (L, GLA_V, D), GLA_V ** -0.5),
        "w_branch_b": nrm(ks[11], (L, SGU_W, D), SGU_W ** -0.5),
        "w_out": nrm(ks[12], (L, D, D), D ** -0.5),
        "norm2_g": 1.0 + nrm(ks[13], (L, D), 0.02),
        "peer_wq": nrm(ks[14], (L, D, PEER_HEADS * PEER_DKEY), D ** -0.5),
        "peer_k1": nrm(ks[15], (L, PEER_NKEYS, PEER_DKEY // 2), (PEER_DKEY // 2) ** -0.5),
        "peer_k2": nrm(ks[16], (L, PEER_NKEYS, PEER_DKEY // 2), (PEER_DKEY // 2) ** -0.5),
        "peer_u": nrm(ks[17], (L, PEER_EXPERTS, D), D ** -0.5),
        "peer_v": nrm(ks[18], (L, PEER_EXPERTS, D), PEER_HEADS ** -0.5),
        "final_g": 1.0 + nrm(ks[19], (D,), 0.02),
    }

def first_block(x, norm1_g, w_in, w_gate_up, b_gate, gla_norm_g, sgu_ln_g, sgu_ln_b, sgu_w, sgu_b,
              w_branch_a, w_branch_b, w_out, norm2_g, peer_wq, peer_k1, peer_k2, peer_u, peer_v,
              final_g):
    offs = np.cumsum(IN_COLS)[:-1].tolist()
    h = x
    for l in range(DEPTH):
        n1 = rmsnorm(h, norm1_g[l])
        proj = n1 @ w_in[l]
        q, k, v, r, a_lr, su, sv, ga, gb = jnp.split(proj, offs, axis=-1)
        y_a = gla_branch(q, k, v, r, a_lr, w_gate_up[l], b_gate[l], gla_norm_g[l])
        su = jax.nn.gelu(su)
        sv = jax.nn.gelu(sv)
        y_b = sgu_branch(su, sv, sgu_ln_g[l], sgu_ln_b[l], sgu_w[l], sgu_b[l])
        merged = (jax.nn.sigmoid(ga) * (y_a @ w_branch_a[l])
                  + jax.nn.sigmoid(gb) * (y_b @ w_branch_b[l]))
        h = h + merged @ w_out[l]
        n2 = rmsnorm(h, norm2_g[l])
        h = h + peer(n2, peer_wq[l], peer_k1[l], peer_k2[l], peer_u[l], peer_v[l])
    return rmsnorm(h, final_g)


GRID_W = 64
CTX_LEN = 256
RET_HEADS = 4
RET_DK = 256
RET_DV = 512
RET_CHUNK = 128
FOURIER_GROUPS = 4
FOURIER_DG = 256
D_FF = 2816
ROPE_BASE = 10000.0
N_MOD = 9

RET_QK = RET_HEADS * RET_DK
RET_V = RET_HEADS * RET_DV
FOURIER_W = FOURIER_GROUPS * FOURIER_DG
IN_COLS_2 = 2 * RET_QK + 2 * RET_V + FOURIER_W + 2 * D_MODEL
SPLITS = (RET_QK, 2 * RET_QK, 2 * RET_QK + RET_V, 2 * RET_QK + 2 * RET_V,
          2 * RET_QK + 2 * RET_V + FOURIER_W, 2 * RET_QK + 2 * RET_V + FOURIER_W + D_MODEL)


def rmsnorm_2(x, w):
    xf = x.astype(jnp.float32)
    y = xf * lax.rsqrt(jnp.mean(xf * xf, axis=-1, keepdims=True) + EPS)
    return (y * w.astype(jnp.float32)).astype(x.dtype)

def modulate(h, shift, scale):
    return h * (1 + scale) + shift

def swiglu(h, w13, w2):
    a, b = jnp.split(h @ w13, 2, axis=-1)
    return (jax.nn.silu(a) * b) @ w2

def heads(a, dh):
    B, L, _ = a.shape
    return a.reshape(B, L, -1, dh).transpose(0, 2, 1, 3)

def project(h, w_in):
    u = h @ w_in
    q, k, v, g, f, ga, gf = jnp.split(u, SPLITS, axis=-1)
    q = heads(q, RET_DK).astype(jnp.float32) * (RET_DK ** -0.5)
    k = heads(k, RET_DK).astype(jnp.float32)
    v = heads(v, RET_DV).astype(jnp.float32)
    return q, k, v, g, f, ga, gf

def rope_2d(a, rows):
    row = jnp.repeat(jnp.arange(rows, dtype=jnp.float32), GRID_W)
    col = jnp.tile(jnp.arange(GRID_W, dtype=jnp.float32), rows)
    n_freq = RET_DK // 4
    inv = ROPE_BASE ** (-jnp.arange(n_freq, dtype=jnp.float32) / n_freq)
    ang = jnp.concatenate([row[:, None] * inv, col[:, None] * inv], axis=-1)
    cos, sin = jnp.cos(ang), jnp.sin(ang)
    a1, a2 = a[..., 0::2], a[..., 1::2]
    return jnp.stack([a1 * cos - a2 * sin, a1 * sin + a2 * cos], axis=-1).reshape(a.shape)

def retention_scan(q, k, v, log_gamma, s0):
    B, H, L, dk = q.shape
    dv = v.shape[-1]
    C = RET_CHUNK
    n = L // C
    idx = jnp.arange(C, dtype=jnp.float32)
    lg = log_gamma[:, None]
    diff = idx[:, None] - idx[None, :]
    decay_intra = jnp.where(diff >= 0, jnp.exp(lg[:, :, None] * jnp.maximum(diff, 0.0)), 0.0)
    xi = jnp.exp(lg * (idx + 1.0))
    zeta = jnp.exp(lg * (C - 1.0 - idx))
    g_chunk = jnp.exp(log_gamma * C)

    def to_chunks(a):
        return jnp.moveaxis(a.reshape(B, H, n, C, a.shape[-1]), 2, 0)

    def step(s, qkv):
        qc, kc, vc = qkv
        sc = jnp.einsum('bhid,bhjd->bhij', qc, kc) * decay_intra
        o = (jnp.einsum('bhij,bhjv->bhiv', sc, vc)
             + jnp.einsum('bhid,bhdv->bhiv', qc, s) * xi[None, :, :, None])
        s = s * g_chunk[None, :, None, None] + jnp.einsum('bhjd,bhjv->bhdv', kc * zeta[None, :, :, None], vc)
        return s, o

    s, o = lax.scan(step, s0, (to_chunks(q), to_chunks(k), to_chunks(v)))
    o = jnp.moveaxis(o, 0, 2).reshape(B, H, L, dv)
    return o, s

def bidir_retention(q, k, v, lg_f, lg_b, s_f0, s_b0):
    o_f, s_f = retention_scan(q, k, v, lg_f, s_f0)
    flip = lambda a: jnp.flip(a, axis=2)
    o_b, s_b = retention_scan(flip(q), flip(k), flip(v), lg_b, s_b0)
    return o_f + flip(o_b), s_f, s_b

def retention_out(o, g, gn_w, p_ret):
    mu = jnp.mean(o, axis=-1, keepdims=True)
    var = jnp.mean(jnp.square(o - mu), axis=-1, keepdims=True)
    on = (o - mu) * lax.rsqrt(var + EPS)
    B, H, L, dv = o.shape
    on = on.transpose(0, 2, 1, 3).reshape(B, L, H * dv).astype(g.dtype) * gn_w
    return (jax.nn.silu(g) * on) @ p_ret

def fourier_branch(f, p_four):
    B, L, _ = f.shape
    fg = f.reshape(B, L, FOURIER_GROUPS, FOURIER_DG).astype(jnp.float32)
    mixed = jnp.fft.fft2(fg, axes=(1, 3), norm="ortho").real
    return mixed.reshape(B, L, FOURIER_W).astype(f.dtype) @ p_four

def merge(r, fo, ga, gf, w_out):
    return (jax.nn.sigmoid(ga) * r + jax.nn.sigmoid(gf) * fo) @ w_out

def second_inputs(seed: int = 0) -> dict:
    key = jax.random.key(seed)
    ks = jax.random.split(key, 24)

    def w(k, shape, fan_in, scale=1.0):
        return jax.random.normal(k, shape, jnp.float32) * (scale * fan_in ** -0.5)

    def gain(k, shape):
        return 1.0 + 0.02 * jax.random.normal(k, shape, jnp.float32)

    decay_base = jnp.asarray(np.log(2.0 ** (5 + np.arange(RET_HEADS)) - 1.0).astype(np.float32))
    return {
        "x": jax.random.normal(ks[0], (BATCH, SEQ, D_MODEL), jnp.float32),
        "c": jax.random.normal(ks[1], (BATCH, D_MODEL), jnp.float32),
        "ctx": jax.random.normal(ks[2], (BATCH, CTX_LEN, D_MODEL), jnp.float32),
        "c_ctx": 0.5 * jax.random.normal(ks[3], (D_MODEL,), jnp.float32),
        "w_ada": w(ks[4], (DEPTH, D_MODEL, N_MOD * D_MODEL), D_MODEL, 0.5),
        "b_ada": 0.02 * jax.random.normal(ks[5], (DEPTH, N_MOD * D_MODEL), jnp.float32),
        "norm_ffn1": gain(ks[6], (DEPTH, D_MODEL)),
        "w13_ffn1": w(ks[7], (DEPTH, D_MODEL, 2 * D_FF), D_MODEL),
        "w2_ffn1": w(ks[8], (DEPTH, D_FF, D_MODEL), D_FF),
        "norm_mix": gain(ks[9], (DEPTH, D_MODEL)),
        "w_in": w(ks[10], (DEPTH, D_MODEL, IN_COLS_2), D_MODEL),
        "decay_fwd": decay_base[None, :] + 0.05 * jax.random.normal(ks[11], (DEPTH, RET_HEADS), jnp.float32),
        "decay_bwd": decay_base[None, :] + 0.05 * jax.random.normal(ks[12], (DEPTH, RET_HEADS), jnp.float32),
        "ret_gn_w": gain(ks[13], (DEPTH, RET_V)),
        "p_ret": w(ks[14], (DEPTH, RET_V, D_MODEL), RET_V),
        "p_four": w(ks[15], (DEPTH, FOURIER_W, D_MODEL), FOURIER_W),
        "w_out": w(ks[16], (DEPTH, D_MODEL, D_MODEL), D_MODEL),
        "norm_ffn2": gain(ks[17], (DEPTH, D_MODEL)),
        "w13_ffn2": w(ks[18], (DEPTH, D_MODEL, 2 * D_FF), D_MODEL),
        "w2_ffn2": w(ks[19], (DEPTH, D_FF, D_MODEL), D_FF),
        "norm_final": gain(ks[20], (D_MODEL,)),
    }

def second_block(x, c, ctx, c_ctx, w_ada, b_ada, norm_ffn1, w13_ffn1, w2_ffn1, norm_mix, w_in,
              decay_fwd, decay_bwd, ret_gn_w, p_ret, p_four, w_out, norm_ffn2, w13_ffn2, w2_ffn2,
              norm_final):
    B, L, _ = x.shape
    rows = L // GRID_W
    for l in range(DEPTH):
        last = l == DEPTH - 1
        mod_x = (jax.nn.silu(c) @ w_ada[l] + b_ada[l])[:, None, :]
        mod_c = (jax.nn.silu(c_ctx) @ w_ada[l] + b_ada[l])[None, None, :]
        sh1x, sc1x, g1x, sh2x, sc2x, g2x, sh3x, sc3x, g3x = jnp.split(mod_x, N_MOD, axis=-1)
        sh1c, sc1c, g1c, sh2c, sc2c, g2c, sh3c, sc3c, g3c = jnp.split(mod_c, N_MOD, axis=-1)

        x = x + 0.5 * g1x * swiglu(modulate(rmsnorm_2(x, norm_ffn1[l]), sh1x, sc1x), w13_ffn1[l], w2_ffn1[l])
        ctx = ctx + 0.5 * g1c * swiglu(modulate(rmsnorm_2(ctx, norm_ffn1[l]), sh1c, sc1c), w13_ffn1[l], w2_ffn1[l])

        lg_f = jax.nn.log_sigmoid(decay_fwd[l].astype(jnp.float32))
        lg_b = jax.nn.log_sigmoid(decay_bwd[l].astype(jnp.float32))

        qc, kc, vc, gc, fc, gac, gfc = project(modulate(rmsnorm_2(ctx, norm_mix[l]), sh2c, sc2c), w_in[l])
        zero = jnp.zeros((ctx.shape[0], RET_HEADS, RET_DK, RET_DV), jnp.float32)
        o_c, s_f, s_b = bidir_retention(qc, kc, vc, lg_f, lg_b, zero, zero)

        qx, kx, vx, gx, fx, gax, gfx = project(modulate(rmsnorm_2(x, norm_mix[l]), sh2x, sc2x), w_in[l])
        qx = rope_2d(qx, rows)
        kx = rope_2d(kx, rows)
        o_x, _, _ = bidir_retention(qx, kx, vx, lg_f, lg_b, s_f, s_b)
        y_x = merge(retention_out(o_x, gx, ret_gn_w[l], p_ret[l]), fourier_branch(fx, p_four[l]), gax, gfx, w_out[l])
        x = x + g2x * y_x

        x = x + 0.5 * g3x * swiglu(modulate(rmsnorm_2(x, norm_ffn2[l]), sh3x, sc3x), w13_ffn2[l], w2_ffn2[l])

        if not last:
            y_c = merge(retention_out(o_c, gc, ret_gn_w[l], p_ret[l]), fourier_branch(fc, p_four[l]), gac, gfc, w_out[l])
            ctx = ctx + g2c * y_c
            ctx = ctx + 0.5 * g3c * swiglu(modulate(rmsnorm_2(ctx, norm_ffn2[l]), sh3c, sc3c), w13_ffn2[l], w2_ffn2[l])
    return rmsnorm_2(x, norm_final)


def setup_inputs(seed=0):
    out = dict(first_inputs(seed))
    for name, value in second_inputs(seed + 1).items():
        if name != "x":
            out[name + "_2"] = value
    return out


def reference(
    x, norm1_g, w_in, w_gate_up, b_gate, gla_norm_g, sgu_ln_g, sgu_ln_b, sgu_w, sgu_b,
    w_branch_a, w_branch_b, w_out, norm2_g, peer_wq, peer_k1, peer_k2, peer_u, peer_v, final_g,
    c_2, ctx_2, c_ctx_2, w_ada_2, b_ada_2, norm_ffn1_2, w13_ffn1_2, w2_ffn1_2, norm_mix_2,
    w_in_2, decay_fwd_2, decay_bwd_2, ret_gn_w_2, p_ret_2, p_four_2, w_out_2, norm_ffn2_2,
    w13_ffn2_2, w2_ffn2_2, norm_final_2,
):
    x = first_block(
        x, norm1_g, w_in, w_gate_up, b_gate, gla_norm_g, sgu_ln_g, sgu_ln_b, sgu_w, sgu_b,
        w_branch_a, w_branch_b, w_out, norm2_g, peer_wq, peer_k1, peer_k2, peer_u, peer_v,
        final_g,
    )
    return second_block(
        x, c_2, ctx_2, c_ctx_2, w_ada_2, b_ada_2, norm_ffn1_2, w13_ffn1_2, w2_ffn1_2,
        norm_mix_2, w_in_2, decay_fwd_2, decay_bwd_2, ret_gn_w_2, p_ret_2, p_four_2, w_out_2,
        norm_ffn2_2, w13_ffn2_2, w2_ffn2_2, norm_final_2,
    )


_drawn_inputs = setup_inputs


def setup_inputs(seed=0):
    import zlib

    import numpy as np

    out = dict(_drawn_inputs(seed))
    spreads = {}
    factors = {'gla_norm_g': 3.865,
     'sgu_ln_g': 6.014,
     'sgu_ln_b': 6.093,
     'sgu_b': 3.85,
     'final_g': 2.771,
     'c_ctx_2': 3.789,
     'b_ada_2': 3.154,
     'norm_ffn1_2': 8.0,
     'norm_mix_2': 8.0,
     'ret_gn_w_2': 25.823,
     'norm_ffn2_2': 31.095,
     'norm_final_2': 8.103}
    for name, (base, spread) in spreads.items():
        noise = np.random.default_rng([zlib.crc32(name.encode()), seed]).standard_normal(out[name].shape)
        drawn = base * np.exp(spread * noise) if base else spread * noise
        out[name] = __import__('jax').numpy.asarray(drawn.astype(out[name].dtype))
    for name, factor in factors.items():
        out[name] = (out[name] * factor).astype(out[name].dtype)
    return out
```

```python
import concourse.bass as bass
from concourse import mybir
from contextlib import ExitStack

F32 = mybir.dt.float32
F32R = mybir.dt.float32r
U32 = mybir.dt.uint32
ACT = mybir.ActivationFunctionType
ALU = mybir.AluOpType
AXX = mybir.AxisListType.X

P = 128
D = 1024
KB = D // P
T = 256
TT = T // P
EPS = 1e-6
HEADS = 4
CHUNK = 64
NCK = T // CHUNK
TAU = 16.0
PEER_HEADS, TOPK, NKEYS = 8, 16, 128
SLOTS = PEER_HEADS * TOPK
NEG = -3.0e38
FF = 2816 // P
RH, RV = 4, 512
N_MOD = 9
MODB = N_MOD * KB

ORDER = [
    ("alr", 1),
    ("tok", 12),
    ("feat", 28),
    ("branch", 8),
    ("wout", 8),
    ("wq", 16),
    ("ada", MODB),
    ("peer", 256),
    ("up1", 2 * FF), ("down1", FF),
    ("heads", 12 * RH),
    ("four", 8),
    ("gates", 16),
    ("proj", 24),
    ("wout2", 8),
    ("up2", 2 * FF), ("down2", FF),
]
C0, _n = {}, 0
for _name, _count in ORDER:
    C0[_name] = _n
    _n += _count
NCH = _n

COLS = {}
_n = 0
for _name, _count in [("norm1", 8), ("norm2", 8), ("final", 8), ("gla", 4), ("ffn1", 8), ("mix", 8),
                      ("ffn2", 8), ("last", 8), ("gn", 16), ("bada", MODB)]:
    COLS[_name] = _n
    _n += _count
NCOLS = _n


def at(first, step, it):
    return first if it is None else it * step + first


class Tally:

    def __init__(self, eng, sem, spacer=None):
        self.eng, self.sem, self.spacer, self.n, self.it, self.per = eng, sem, spacer, 0, None, 0

    def link(self, ins):
        self.n += 1
        ins.then_inc(self.sem, 1)
        self.eng.wait_ge(self.sem, at(self.n, self.per, self.it))

    def apart(self):
        self.eng.sem_inc(self.spacer, 1)

    def begin(self, it, per):
        self.it, self.per, self.start = it, per, self.n

    def end(self, rounds):
        assert self.n - self.start == self.per, (self.n - self.start, self.per)
        self.n = self.start + self.per * rounds
        self.it, self.per = None, 0


class Sems(dict):

    def __init__(self, nc, ctx):
        self.nc, self.ctx = nc, ctx

    def __missing__(self, name):
        self[name] = self.ctx.enter_context(self.nc.semaphore(name))
        return self[name]


def build(nc, a, out):
    ctx = ExitStack()
    with ctx:
        s = Sems(nc, ctx)
        base = 16512
        place = [0]

        def sb(name, shape, offset=None, dt=F32):
            size = 4
            for d in shape[1:]:
                size *= d
            if offset is None:
                offset = place[0]
            place[0] = offset + (size + 31) // 32 * 32
            return nc.alloc_sbuf_tensor_at(name, shape, dt, offset=base + offset)

        RAW = sb("RAW", [P, 4, 1024], 0)
        WH = sb("WH", [P, 4, 1024], dt=F32R)
        WL = sb("WL", [P, 4, 1024], dt=F32R)
        H = sb("H", [P, KB, T])
        XH = sb("XH", [P, KB, T], dt=F32R)
        XL = sb("XL", [P, KB, T], dt=F32R)
        AH = sb("AH", [P, 2, T], dt=F32R)
        AL = sb("AL", [P, 2, T], dt=F32R)
        REG = place[0]
        G = sb("G", [P, NKEYS, T])
        CL = sb("CL", [P, NCOLS])
        MOD = sb("MOD", [P, MODB, 2])
        SCG = sb("SCG", [P, 3, KB, 2])
        GH = sb("GH", [P, 2, KB, 2])
        ONES = sb("ONES", [P, P])
        ZR = sb("ZR", [P, P])
        EPSC = sb("EPSC", [P, 1])
        LGD = sb("LGD", [P, 4, 8])
        CS = sb("CS", [P, KB, 2])
        assert base + place[0] <= nc.sbuf_usable_end

        PROJ = sb("PROJ", [P, 28, T], REG)
        KT = sb("KT", [P, TT, 512])
        VT = sb("VT", [P, TT, 512])
        SV = sb("SV", [P, TT, 512])
        ALR = sb("ALR", [32, T])
        WA2 = sb("WA2", [17, 512])
        LG1 = sb("LG1", [P, TT, 512])
        LOGA = sb("LOGA", [P, TT, 512])
        EXS = sb("EXS", [P, TT, 512])
        ST = sb("ST", [P, NCK, HEADS * P])
        DEC = sb("DEC", [P, HEADS, NCK])
        OG = sb("OG", [P, HEADS, T])
        RMS2 = sb("RMS2", [P, HEADS, T])
        SQ2 = sb("SQ2", [P, HEADS, T])
        TMP8 = sb("TMP8", [P, KB, T])
        RMS = sb("RMS", [P, T])
        UM = sb("UM", [P, P])
        BONES = sb("BONES", [P, 2])
        WST = sb("WST", [P, 4, P])
        BS = sb("BS", [1, 512])
        LNG = sb("LNG", [P, 512])
        LNB = sb("LNB", [P, 512])
        ST6 = sb("ST6", [P, TT, 6])
        MV = sb("MV", [P, TT, 2])
        TMPM = sb("TMPM", [P, 2, T])
        MG = sb("MG", [P, KB, T])
        IDENT = sb("IDENT", [P, P])
        K12T = sb("K12T", [P, 2, P])
        QT = sb("QT", [P, 4, T])
        assert place[0] <= REG + 131072
        MH = sb("MH", [P, KB, T], REG + 28672, dt=F32R)
        ML = sb("ML", [P, KB, T], dt=F32R)
        SC = sb("SC", [P, 16, TT, NKEYS], REG)
        STG = sb("STG", [P, 2, TT, NKEYS])
        STG2 = sb("STG2", [P, 2, TT, NKEYS])
        V16 = sb("V16", [P, 2, TT, TOPK])
        I16 = sb("I16", [P, 2, TT, TOPK], dt=U32)
        CAND = sb("CAND", [P, TT, TOPK, TOPK], REG + 28672)
        CAND2 = sb("CAND2", [P, TT, TOPK, TOPK])
        CV = sb("CV", [P, TT, TOPK])
        CI = sb("CI", [P, TT, TOPK], dt=U32)
        VAL = sb("VAL", [P, TT, PEER_HEADS, TOPK])
        CIU = sb("CIU", [P, TT, PEER_HEADS, TOPK], dt=U32)
        IAU = sb("IAU", [P, 2, TT, PEER_HEADS, TOPK], dt=U32)
        IAF = sb("IAF", [P, 2, TT, PEER_HEADS, TOPK])
        IF = sb("IF", [P, 2, TT, PEER_HEADS, TOPK])
        EQ = sb("EQ", [P, PEER_HEADS, TOPK, TOPK])
        SEL = sb("SEL", [P, 3, TT, PEER_HEADS, TOPK])
        GSUM = sb("GSUM", [P, TT, PEER_HEADS])
        IOTA16 = sb("IOTA16", [P, TOPK])
        assert place[0] <= REG + 65536
        SLT = sb("SLT", [P, 3, T], 16384)
        IOTA = sb("IOTA", [P, P])
        OJ = sb("OJ", [P, 4, 4, P])
        OI = sb("OI", [P, 4, 4, P])
        SJ = sb("SJ", [P, 4, 4])

        HX = sb("HX", [P, KB, 2 * T], 57344)
        XH2 = sb("XH2", [P, KB * 2 * T], REG, dt=F32R)
        XL2 = sb("XL2", [P, KB * 2 * T], dt=F32R)
        R2 = place[0]
        HIDH = sb("HIDH", [P, FF, 2 * T], R2, dt=F32R)
        HIDL = sb("HIDL", [P, FF, 2 * T], dt=F32R)
        TA = sb("TA", [P, 2, 2 * T])
        HT = sb("HT", [P, 2, 2 * T])
        TMP16 = sb("TMP16", [P, KB, 2 * T], R2)
        RMS5 = sb("RMS5", [P, 2 * T])
        YRH = sb("YRH", [P, 16, T], R2, dt=F32R)
        YRL = sb("YRL", [P, 16, T], dt=F32R)
        GS = sb("GS", [P, 16, T])
        R3 = place[0]
        QR = sb("QR", [P, 2, T])
        KR = sb("KR", [P, 2, 2 * T])
        VR = sb("VR", [P, 4, RV])
        SG = sb("SG", [P, 4, T])
        EF = sb("EF", [P, 4, T])
        EB = sb("EB", [P, 4, T])
        PT = sb("PT", [P, 4, T])
        ON = sb("ON", [P, TT, RV])
        YT = sb("YT", [P, 4, T])
        RT = sb("RT", [P, 4, T])
        MASK = sb("MASK", [P, 2, 2, T])
        ROPE = sb("ROPE", [P, 2, T])
        assert place[0] <= REG + 131072
        FT = sb("FT", [P, TT, D], R3)
        AB = sb("AB", [P, KB, 2 * T])
        DFTL = sb("DFTL", [P, TT, 2 * T])
        DFTD = sb("DFTD", [P, 2, 2, T])
        YFH = sb("YFH", [P, KB, T], dt=F32R)
        YFL = sb("YFL", [P, KB, T], dt=F32R)
        assert place[0] <= REG + 131072
        MG2 = sb("MG2", [P, KB, T], R3)
        TMP2 = sb("TMP2", [P, 2, T])
        DIST = sb("DIST", [P, 2, 4, T], 49152)
        IDENT2 = sb("IDENT2", [P, P], 73728)
        OST6 = sb("OST6", [P, TT, 6])
        OMV = sb("OMV", [P, TT, 2])
        assert place[0] <= REG

        ps = ctx.enter_context(nc.psum_tensor("ps", [P, 8, 512], F32))

        def col(name, k):
            return CL[:, COLS[name] + k:COLS[name] + k + 1]

        XH2_8 = XH2[:, 0:KB * T].rearrange("p (k t) -> p k t", k=KB)
        XL2_8 = XL2[:, 0:KB * T].rearrange("p (k t) -> p k t", k=KB)
        XH2_16 = XH2[:, :].rearrange("p (k t) -> p k t", k=KB)
        XL2_16 = XL2[:, :].rearrange("p (k t) -> p k t", k=KB)

        landed = [s[f"raw_landed{j}"] for j in range(4)]
        hi_ready = s["hi_ready"]
        lo_ready = s["lo_ready"]
        chunk_done = s["chunk_done"]
        ring_evac = s["ring_evac"]
        ADA, ADA_END = C0["ada"], C0["ada"] + MODB

        def split_index(c):
            return c if c < ADA else c - MODB

        U_ALR, U_FEAT = 3, 4
        U_BRANCH = U_FEAT + 28
        U_WOUT = U_BRANCH + 8
        U_WQ = U_WOUT + 8
        U_GATES = U_WQ + 16
        U_PROJ = U_GATES + 16
        U_WOUT2 = U_PROJ + 8
        U_END = U_WOUT2 + 8

        block = ctx.enter_context(nc.Block())

        @block.sync
        def _(sp):
            def load(slot, c, count=0):
                sp.dma_start(RAW[:, slot, :], a["wstream"][c]).then_inc(landed[slot], 16)

            sp.dma_start(H[:, :, :], a["xT"]).then_inc(s["x_landed"], 16)
            for c in range(4):
                load(c, c)
            for dst, name in ((CL[:, :], "cols"), (WA2[:, :], "wa2b"), (UM[:, :], "umat"),
                              (BONES[:, :], "bones"), (WST[:, :, :], "wsT"), (BS[:, :], "bs"),
                              (LNG[:, :], "lng"), (LNB[:, :], "lnb"), (IDENT[:, :], "ident"),
                              (K12T[:, :, :], "k12T"), (CS[:, :, :], "cT"), (LGD[:, 0, :], "decays")):
                sp.dma_start(dst, a[name]).then_inc(s["const_landed"], 16)
            with sp.Fori(0, 18) as it:
                for j in range(4):
                    sp.wait_ge(lo_ready, at(j + 1, 4, it))
                    load(j, it * 4 + (j + 4))
            sp.wait_ge(lo_ready, 73)
            load(0, 76)
            with sp.Fori(0, MODB // 4) as it:
                for j in range(4):
                    sp.wait_ge(chunk_done, at(74 + j, 4, it))
                    load((77 + j) % 4, it * 4 + (77 + j))
            with sp.Fori(0, (NCH - 149) // 4) as it:
                for j in range(4):
                    sp.wait_ge(lo_ready, at(149 + j - 3 - MODB, 4, it))
                    load((149 + j) % 4, it * 4 + (149 + j))
            sp.wait_ge(s["norm_out"], 7)
            sp.dma_start(out, HX[:, :, 0:T]).then_inc(s["out_written"], 16)
            sp.wait_ge(s["out_written"], 16)

        @block.gpsimd
        def _(pool):
            for n, (dst, value) in enumerate(((ONES, 1.0), (ZR, 0.0), (EPSC, EPS), (ALR, 1.0))):
                pool.memset(dst[:, :], value).then_inc(s["pool_consts"], 1)
                pool.wait_ge(s["pool_consts"], n + 1)
            pool.wait_ge(s["const_landed"], 16 * 12)
            pool.memset(WST[64:128, :, 0:64], 0.0).then_inc(s["pool_consts"], 1)
            pool.wait_ge(ring_evac, U_WOUT)
            pool.iota(IOTA16[:, :], [[1, TOPK]], 0, 0, allow_small_or_imprecise_dtypes=True).then_inc(s["iota_ready"], 1)
            pool.wait_ge(s["iota_ready"], 1)
            pool.wait_ge(chunk_done, ADA)
            pool.iota(IOTA[:, :], [[1, P]], 0, 0, allow_small_or_imprecise_dtypes=True).then_inc(s["iota_ready"], 1)
            pool.wait_ge(s["iota_ready"], 2)
            pool.wait_ge(s["slots_ready"], 1)
            with pool.Fori(0, T // 16) as it:
                for q in range(4):
                    pool.wait_ge(s["onehot_used"], at(q + 1, 4, it))
                    pool.tensor_copy(SJ[:, q, :], SLT[:, 1, bass.ds(it * 16 + 4 * q, 4)]).then_inc(s["sj_ready"], 1)
                    pool.wait_ge(s["sj_ready"], at(q + 1, 4, it))
                    pool.sem_inc(s["pool_spacer"], 1)
                    for t in range(4):
                        ins = pool.tensor_scalar(OJ[:, q, t, :], IOTA[:, :], SJ[:, q, t:t + 1], None, ALU.is_equal)
                    ins.then_inc(s["oj_ready"], 1)
            pool.wait_ge(chunk_done, C0["up1"])
            pool.dma_start(HX[:, :, T:2 * T], a["ctxT"]).then_inc(s["ctx_landed"], 16)
            pool.dma_start(IDENT2[:, :], a["ident"]).then_inc(s["tables_landed"], 16)
            pool.wait_ge(s["norm_out"], 3)
            pool.dma_start(DIST[:, :, :, :], a["dist"]).then_inc(s["tables_landed"], 16)
            pool.wait_ge(chunk_done, C0["heads"])
            pool.dma_start(MASK[:, :, :, :], a["mask"]).then_inc(s["tables_landed"], 16)
            pool.dma_start(ROPE[:, :, :], a["rope"]).then_inc(s["tables_landed"], 16)
            pool.wait_ge(s["yr_ready"], RH)
            pool.dma_start(DFTL[:, :, :], a["dftl"]).then_inc(s["tables_landed"], 16)
            pool.dma_start(DFTD[:, :, :, :], a["dftd"]).then_inc(s["tables_landed"], 16)

        @block.scalar
        def _(act):
            step = Tally(act, s["act_step"])

            def split_hi(c, it=None, n=0):
                slot = c % 4
                act.wait_ge(landed[slot], at(16 * (c // 4 + 1), 4 * n, it))
                if c >= 4:
                    act.wait_ge(chunk_done, at(c - 3, n, it))
                act.activation(WH[:, slot, :], RAW[:, slot, :], ACT.Copy).then_inc(hi_ready, 1)

            def norm(n, src, tmp, rms, xh, shift=None, last=False):
                act.activation(tmp, src, ACT.Square).then_inc(s["norm_sq"], 1)
                act.wait_ge(s["norm_sum"], n + 1)
                act.activation(rms, ps[:, 4, 0:rms.shape[1]], ACT.Sqrt, bias=EPSC[:, 0:1],
                               scale=1.0 / D).then_inc(s["norm_rms"], 1)
                if last:
                    return
                act.wait_ge(s["norm_out"], n + 1)
                if shift is None:
                    act.activation(xh, tmp, ACT.Copy).then_inc(s["norm_hi"], 1)
                    return
                for half in range(rms.shape[1] // T):
                    for k in range(KB):
                        cols = slice(half * T, half * T + T)
                        ins = act.activation(xh[:, k, cols], tmp[:, k, cols], ACT.Identity,
                                             bias=shift(k, half))
                ins.then_inc(s["norm_hi"], 1)

            act.wait_ge(s["x_landed"], 16)
            act.wait_ge(s["pool_consts"], 5)
            norm(0, H[:, :, :], TMP8[:, :, :], RMS[:, :], XH[:, :, :])
            split_hi(0)
            split_hi(1)
            for c in range(0, 13):
                split_hi(c + 2)
                if c in (4, 8, 12):
                    n = c // 4 - 1
                    act.wait_ge(chunk_done, c + 1)
                    act.activation((KT, VT, SV)[n][:, :, :], ps[:, 4 + 2 * (n % 2):6 + 2 * (n % 2), :],
                                   (ACT.Copy, ACT.Copy, ACT.Gelu_apprx_tanh)[n]).then_inc(s["tok_ready"], 1)
            with act.Fori(0, 7) as it:
                for j in range(4):
                    split_hi(C0["feat"] + j + 2, it, 4)
                    act.wait_ge(chunk_done, at(C0["feat"] + j + 1, 4, it))
                    act.activation(PROJ[:, bass.ds(it * 4 + j, 1), :], ps[:, (U_FEAT + j) % 4, 0:T].unsqueeze(1),
                                   ACT.Copy).then_inc(ring_evac, 1)
            act.wait_ge(s["z_ready"], 1)
            step.link(act.activation(LG1[:, :, :], ps[:, 4:6, :], ACT.Abs))
            step.link(act.activation(LG1[:, :, :], LG1[:, :, :], ACT.Exp, scale=-1.0))
            act.activation(LG1[:, :, :], LG1[:, :, :], ACT.Ln, bias=ONES[:, 0:1]).then_inc(s["ln_ready"], 1)
            act.wait_ge(s["suffix_ready"], 1)
            act.activation(EXS[:, :, :], ps[:, 6:8, :], ACT.Exp).then_inc(s["exs_ready"], 1)
            act.activation(DEC[:, :, :], ps[:, 4, 0:16].rearrange("p (h c) -> p h c", h=HEADS),
                           ACT.Exp).then_inc(s["exs_ready"], 1)
            act.wait_ge(ring_evac, U_BRANCH)
            act.activation(PROJ[:, 4:8, :], PROJ[:, 4:8, :], ACT.Silu).then_inc(s["r_ready"], 1)
            act.activation(PROJ[:, 8:12, :], PROJ[:, 8:12, :], ACT.Gelu_apprx_tanh).then_inc(s["su_ready"], 1)
            act.activation(PROJ[:, 12:28, :], PROJ[:, 12:28, :], ACT.Sigmoid).then_inc(s["sig_ready"], 1)
            act.wait_ge(s["sgu_var"], 1)
            act.activation(MV[:, :, 1:2], MV[:, :, 1:2], ACT.Sqrt, bias=EPSC[:, 0:1]).then_inc(s["sgu_std"], 1)
            act.wait_ge(s["o_ready"], 1)
            o_ps = ps[:, 4:6, :].rearrange("p b (h t) -> p (b h) t", t=T)
            act.activation(OG[:, :, :], o_ps, ACT.Copy, scale=float(P) ** -0.5).then_inc(s["og_ready"], 1)
            act.activation(SQ2[:, :, :], o_ps, ACT.Square, scale=float(P) ** -0.5).then_inc(s["og_sq"], 1)
            act.wait_ge(s["og_sum"], 1)
            act.activation(RMS2[:, :, :], ps[:, 6:8, :].rearrange("p b (h t) -> p (b h) t", t=T), ACT.Sqrt,
                           bias=EPSC[:, 0:1], scale=1.0 / P).then_inc(s["og_rms"], 1)
            act.wait_ge(s["ya_ready"], 1)
            act.activation(XH[:, 0:4, :], OG[:, :, :], ACT.Copy).then_inc(s["y_hi"], 1)
            act.wait_ge(s["yb_ready"], 1)
            act.activation(XH[:, 4:8, :], PROJ[:, 8:12, :], ACT.Copy).then_inc(s["y_hi"], 1)
            with act.Fori(0, 2) as it:
                for j in range(4):
                    split_hi(C0["branch"] + j + 2, it, 4)
            act.wait_ge(s["mg_ready"], 1)
            act.activation(MH[:, :, :], MG[:, :, :], ACT.Copy).then_inc(s["m_hi"], 1)
            with act.Fori(0, 2) as it:
                for j in range(4):
                    split_hi(C0["wout"] + j + 2, it, 4)
            act.wait_ge(ring_evac, U_WQ)
            norm(1, H[:, :, :], TMP8[:, :, :], RMS[:, :], XH[:, :, :])

            def query(c, j, it):
                act.wait_ge(chunk_done, at(c + 1, 4, it))
                act.wait_ge(s["scores_ready"], at(j + 1, 4, it))
                act.activation(QT[:, j, :], ps[:, (U_WQ + j) % 4, 0:T], ACT.Copy).then_inc(ring_evac, 1)

            def scores(i, j, it):
                act.wait_ge(s["scores_ready"], at(j + 5, 4, it) if it is not None else i + 5)
                dst = SC[:, bass.ds(it * 4 + j, 1), :, :] if it is not None else SC[:, i:i + 1, :, :]
                act.activation(dst, ps[:, 4 + j, 0:2 * P].rearrange("p (o a k) -> p o a k", o=1, a=TT),
                               ACT.Copy).then_inc(s["sc_ready"], 1)

            act.sem_inc(s["sc_ready"], 4)
            with act.Fori(0, 3) as it:
                for j in range(4):
                    split_hi(C0["wq"] + j + 2, it, 4)
                    query(C0["wq"] + j, j, it)
                    if j:
                        scores(None, j - 1, it)
                scores(None, 3, it)
            for j in range(4):
                c = C0["wq"] + 12 + j
                if c + 2 < ADA:
                    split_hi(c + 2)
                act.wait_ge(chunk_done, c + 1)
                act.wait_ge(s["scores_ready"], 13 + j)
                act.activation(QT[:, j, :], ps[:, (U_WQ + j) % 4, 0:T], ACT.Copy).then_inc(ring_evac, 1)
                if j:
                    scores(11 + j, j - 1, None)
            scores(15, 3, None)
            act.activation(CS[:, :, :], CS[:, :, :], ACT.Silu).then_inc(s["cs_ready"], 1)
            step.link(act.activation(LGD[:, 1, :], LGD[:, 0, :], ACT.Abs))
            step.link(act.activation(LGD[:, 1, :], LGD[:, 1, :], ACT.Exp, scale=-1.0))
            act.activation(LGD[:, 2, :], LGD[:, 1, :], ACT.Ln, bias=ONES[:, 0:1]).then_inc(s["lgd_ready"], 1)
            act.wait_ge(s["vals_ready"], 1)
            act.activation(VAL[:, :, :, :], VAL[:, :, :, :], ACT.Exp).then_inc(s["val_exp"], 1)
            act.wait_ge(s["slots_turned"], 1)
            act.activation(SLT[:, 0:2, :], ps[:, 4, :].rearrange("p (a t) -> p a t", t=T), ACT.Copy)
            act.activation(SLT[:, 2, :], ps[:, 5, 0:T], ACT.Copy).then_inc(s["slots_ready"], 1)
            act.sem_inc(s["g_ready"], 4)
            with act.Fori(0, T // 16) as it:
                for q in range(4):
                    act.wait_ge(s["onehot_used"], at(q + 5, 4, it))
                    act.activation(G[:, :, bass.ds(it * 16 + 4 * q, 4)],
                                   ps[:, q, :].rearrange("p (t i) -> p i t", t=4), ACT.Copy).then_inc(s["g_ready"], 1)

            PC = C0["peer"]

            def expert_hi(e, it=None):
                act.wait_ge(s["gated_ready"], at(e + 1, 4, it))
                if it is not None or e >= 2:
                    act.wait_ge(chunk_done, at(PC + 3 + 2 * (e - 2) + 1, 8, it))
                src = G[:, e, :] if it is None else G[:, bass.ds(it * 4 + e, 1), :]
                dst = AH[:, e % 2, :] if it is None else AH[:, e % 2, :].unsqueeze(1)
                act.activation(dst, src, ACT.Copy).then_inc(s["a_hi"], 1)

            for c in range(4):
                split_hi(PC + c)
            act.wait_ge(chunk_done, PC + 1)
            act.activation(ps[:, 0, 0:T], ps[:, 0, 0:T], ACT.Gelu_apprx_tanh).then_inc(s["gelu_ready"], 1)
            expert_hi(0)

            def pair(e, it=None):
                split_hi(PC + 4 + 2 * e, it, 8)
                act.wait_ge(chunk_done, at(PC + (2 * e if e else 1) + 1, 8, it))
                act.activation(ps[:, (e + 1) % 4, 0:T], ps[:, (e + 1) % 4, 0:T],
                               ACT.Gelu_apprx_tanh).then_inc(s["gelu_ready"], 1)
                split_hi(PC + 5 + 2 * e, it, 8)
                expert_hi(e + 1, it)

            for e in range(2):
                pair(e)
            with act.Fori(0, 31) as it:
                for e in range(2, 6):
                    pair(e, it)
            split_hi(PC + 256)
            act.wait_ge(chunk_done, PC + 2 * 126 + 1)
            act.activation(ps[:, 127 % 4, 0:T], ps[:, 127 % 4, 0:T],
                           ACT.Gelu_apprx_tanh).then_inc(s["gelu_ready"], 1)
            expert_hi(127)
            split_hi(PC + 257)

            act.wait_ge(s["peer_added"], 1)
            norm(2, H[:, :, :], TMP16[:, :, 0:T], RMS5[:, 0:T], None, last=True)

            def ffn(n, up, down, width):
                with act.Fori(0, FF // 2) as it:
                    for f in range(2):
                        c = up + 2 * f
                        split_hi(c + 2, it, 4)
                        split_hi(c + 3, it, 4)
                        act.wait_ge(chunk_done, at(c + 1, 4, it))
                        act.activation(TA[:, f, 0:width], ps[:, 2 * f, 0:width],
                                       ACT.Silu).then_inc(s["ffn_silu"], 1)
                        act.wait_ge(s["ffn_prod"], at(n * FF + f + 3, 2, it))
                        act.activation(HIDH[:, bass.ds(it * 2 + f, 1), 0:width], HT[:, f, 0:width].unsqueeze(1),
                                       ACT.Copy).then_inc(s["ffn_hi"], 1)
                with act.Fori(0, 5) as it:
                    for j in range(4):
                        split_hi(down + j + 2, it, 4)
                for c in range(down + 22, min(down + 24, NCH)):
                    split_hi(c)

            act.wait_ge(s["ctx_landed"], 16)
            act.wait_ge(s["norm_out"], 3)
            norm(3, HX[:, :, :], TMP16[:, :, :], RMS5[:, :], XH2_16,
                 lambda k, half: MOD[:, k, half:half + 1])
            ffn(0, C0["up1"], C0["down1"], 2 * T)
            act.wait_ge(s["hx_ready"], 1)
            norm(4, HX[:, :, :], TMP16[:, :, :], RMS5[:, :], XH2_16,
                 lambda k, half: MOD[:, 24 + k, half:half + 1])

            HC = C0["heads"]
            act.wait_ge(s["tables_landed"], 64)
            act.sem_inc(s["sg_ready"], 1)
            with act.Fori(0, RH) as it:
                act.wait_ge(s["p_ready"], it + 1)
                act.activation(EF[:, :, :], DIST[:, 0, :, :], ACT.Exp, scale=LGD[:, 3, bass.ds(it, 1)]).then_inc(s["decay_exp"], 1)
                act.activation(EB[:, :, :], DIST[:, 1, :, :], ACT.Exp, scale=LGD[:, 3, bass.ds(it + RH, 1)]).then_inc(s["decay_exp"], 1)
                for j in range(4):
                    split_hi(HC + j + 2, it, 12)
                act.wait_ge(chunk_done, at(HC + 4, 12, it))
                act.wait_ge(s["pv_ready"], it + 1)
                act.wait_ge(s["qk_ready"], at(1, 1, it))
                act.activation(KR[:, :, T:2 * T], ps[:, 2:4, T:2 * T], ACT.Copy).then_inc(s["kctx_ready"], 1)
                for j in range(4, 8):
                    split_hi(HC + j + 2, it, 12)
                act.wait_ge(chunk_done, at(HC + 8, 12, it))
                act.activation(VR[:, :, :], ps[:, 4:8, :], ACT.Copy).then_inc(s["v_ready"], 1)
                for j in range(8, 12):
                    split_hi(HC + j + 2, it, 12)
                act.wait_ge(chunk_done, at(HC + 12, 12, it))
                act.wait_ge(s["yt_ready"], it + 1)
                act.activation(SG[:, :, :], ps[:, 2:4, :].rearrange("p b (g t) -> p (b g) t", t=T),
                               ACT.Silu).then_inc(s["sg_ready"], 1)
                act.wait_ge(s["o_var"], at(1, 1, it))
                act.activation(OMV[:, :, 1:2], OMV[:, :, 1:2], ACT.Sqrt, bias=EPSC[:, 0:1]).then_inc(s["o_std"], 1)
                act.wait_ge(s["yt_ready"], at(2, 1, it))
                act.activation(YRH[:, bass.ds(it * 4, 4), :], YT[:, :, :], ACT.Copy).then_inc(s["yr_hi"], 1)
            for c in range(8):
                split_hi(C0["four"] + c + 2)
                if c in (3, 7):
                    n = c // 4
                    act.wait_ge(chunk_done, C0["four"] + c + 1)
                    if n == 0:
                        act.wait_ge(s["yr_ready"], RH)
                    act.activation(FT[:, :, n * 512:n * 512 + 512], ps[:, 4 + 2 * n:6 + 2 * n, :],
                                   ACT.Copy).then_inc(s["ft_ready"], 1)
            with act.Fori(0, 4) as it:
                for j in range(4):
                    split_hi(C0["gates"] + j + 2, it, 4)
                    act.wait_ge(chunk_done, at(C0["gates"] + j + 1, 4, it))
                    act.activation(GS[:, bass.ds(it * 4 + j, 1), :], ps[:, (U_GATES + j) % 4, 0:T].unsqueeze(1),
                                   ACT.Sigmoid).then_inc(ring_evac, 1)
            for n in range(KB):
                act.wait_ge(s["dft_tok"], n + 1)
                act.activation(AB[:, n, :], ps[:, 4 + n % 4, :], ACT.Copy).then_inc(s["ab_ready"], 1)
            act.wait_ge(s["dft_feat"], 1)
            act.activation(YFH[:, :, :], ps[:, 0:4, :].rearrange("p b (g t) -> p (b g) t", t=T),
                           ACT.Copy).then_inc(s["yf_hi"], 1)
            with act.Fori(0, 2) as it:
                for j in range(12):
                    split_hi(C0["proj"] + j + 2, it, 12)
            act.wait_ge(s["mg2_ready"], 1)
            act.activation(XH2_8, MG2[:, :, :], ACT.Copy).then_inc(s["m2_hi"], 1)
            with act.Fori(0, 2) as it:
                for j in range(4):
                    split_hi(C0["wout2"] + j + 2, it, 4)
            act.wait_ge(ring_evac, U_END)
            norm(5, HX[:, :, 0:T], TMP16[:, :, 0:T], RMS5[:, 0:T], XH2_8,
                 lambda k, half: MOD[:, 48 + k, half:half + 1])
            ffn(1, C0["up2"], C0["down2"], T)
            act.wait_ge(s["hx_ready"], 2)
            norm(6, HX[:, :, 0:T], TMP16[:, :, 0:T], RMS5[:, 0:T], None, last=True)

        @block.vector
        def _(dve):
            step = Tally(dve, s["dve_step"], s["dve_spacer"])

            def split_lo(c, it=None, n=0):
                slot = c % 4
                dve.wait_ge(hi_ready, at(split_index(c) + 1, n, it))
                dve.tensor_tensor(WL[:, slot, :], RAW[:, slot, :], WH[:, slot, :].bitcast(F32),
                                  ALU.subtract).then_inc(lo_ready, 1)

            def norm(n, src, tmp, rms, xh, xl, gain, shift=None, dst=None):
                dve.wait_ge(s["norm_rms"], n + 1)
                step.link(dve.reciprocal(rms, rms))
                o = tmp if dst is None else dst
                for half in range(rms.shape[1] // T):
                    for k in range(KB):
                        cols = slice(half * T, half * T + T)
                        ins = dve.scalar_tensor_tensor(o[:, k, cols], src[:, k, cols], gain(k, half),
                                                       rms[:, cols], ALU.mult, ALU.mult)
                ins.then_inc(s["norm_out"], 1)
                if dst is not None:
                    return
                dve.wait_ge(s["norm_hi"], n + 1 - (n > 2))
                if shift is None:
                    dve.tensor_tensor(xl, tmp, xh.bitcast(F32), ALU.subtract).then_inc(s["norm_lo"], 1)
                    return
                for half in range(rms.shape[1] // T):
                    for k in range(KB):
                        cols = slice(half * T, half * T + T)
                        ins = dve.scalar_tensor_tensor(xl[:, k, cols], tmp[:, k, cols], shift(k, half),
                                                       xh[:, k, cols].bitcast(F32), ALU.add, ALU.subtract)
                ins.then_inc(s["norm_lo"], 1)

            dve.wait_ge(s["const_landed"], 16 * 12)
            norm(0, H[:, :, :], TMP8[:, :, :], RMS[:, :], XH[:, :, :], XL[:, :, :],
                 lambda k, half: col("norm1", k))
            split_lo(0)
            split_lo(1)
            for c in range(0, 13):
                split_lo(c + 2)
                if c == 0:
                    dve.wait_ge(s["pool_consts"], 5)
                    dve.wait_ge(chunk_done, 1)
                    dve.tensor_copy(ALR[0:16, :], ps[0:16, 3, 0:T]).then_inc(ring_evac, U_FEAT)
            with dve.Fori(0, 7) as it:
                for j in range(4):
                    split_lo(C0["feat"] + j + 2, it, 4)
            dve.wait_ge(s["tok_ready"], 3)
            for tt in range(TT):
                ins = dve.bn_stats(ST6[:, tt, :], SV[:, tt, :])
            step.link(ins)
            for tt in range(TT):
                ins = dve.bn_aggr(MV[:, tt, :], ST6[:, tt, :])
            ins.then_inc(s["sgu_var"], 1)
            dve.wait_ge(s["ln_ready"], 1)
            dve.scalar_tensor_tensor(LOGA[:, :, :], ps[:, 4:6, :], 0.0, LG1[:, :, :], ALU.min,
                                     ALU.subtract).then_inc(s["loga_ready"], 1)
            dve.wait_ge(s["exs_ready"], 1)
            dve.tensor_tensor(KT[:, :, :], KT[:, :, :], EXS[:, :, :], ALU.mult).then_inc(s["kdec_ready"], 1)
            dve.wait_ge(s["sgu_std"], 1)
            step.link(dve.reciprocal(MV[:, :, 1:2], MV[:, :, 1:2]))
            for tt in range(TT):
                ins = dve.tensor_scalar(SV[:, tt, :], SV[:, tt, :], MV[:, tt, 0:1], MV[:, tt, 1:2],
                                        ALU.subtract, ALU.mult)
            step.link(ins)
            for tt in range(TT):
                ins = dve.tensor_tensor(SV[:, tt, :], SV[:, tt, :], LNG[:, :], ALU.mult)
            step.link(ins)
            for tt in range(TT):
                ins = dve.tensor_tensor(SV[:, tt, :], SV[:, tt, :], LNB[:, :], ALU.add)
            ins.then_inc(s["vn_ready"], 1)
            dve.wait_ge(s["kv_ready"], 1)
            dve.wait_ge(s["exs_ready"], 2)
            step.link(dve.tensor_copy(ST[:, 0, :], ps[:, 0, :]))
            for c in range(1, NCK):
                for h in range(HEADS):
                    hs = slice(h * P, h * P + P)
                    ins = dve.scalar_tensor_tensor(ST[:, c, hs], ST[:, c - 1, hs], DEC[:, h, c:c + 1],
                                                   ps[:, c, hs], ALU.mult, ALU.add)
                if c < NCK - 1:
                    step.link(ins)
            ins.then_inc(s["state_ready"], 1)
            dve.wait_ge(s["mixed_ready"], 1)
            dve.wait_ge(s["su_ready"], 1)
            dve.tensor_tensor(PROJ[:, 8:12, :], PROJ[:, 8:12, :],
                              ps[:, 0:2, :].rearrange("p b (g t) -> p (b g) t", t=T),
                              ALU.mult).then_inc(s["yb_ready"], 1)
            dve.wait_ge(s["og_rms"], 1)
            dve.wait_ge(s["og_ready"], 1)
            step.link(dve.reciprocal(RMS2[:, :, :], RMS2[:, :, :]))
            step.link(dve.tensor_tensor(OG[:, :, :], OG[:, :, :], RMS2[:, :, :], ALU.mult))
            dve.wait_ge(s["r_ready"], 1)
            for h in range(HEADS):
                ins = dve.scalar_tensor_tensor(OG[:, h, :], OG[:, h, :], col("gla", h), PROJ[:, 4 + h, :],
                                               ALU.mult, ALU.mult)
            ins.then_inc(s["ya_ready"], 1)
            dve.wait_ge(s["ya_ready"], 1)
            dve.wait_ge(s["y_hi"], 1)
            dve.tensor_tensor(XL[:, 0:4, :], OG[:, :, :], XH[:, 0:4, :].bitcast(F32), ALU.subtract)
            dve.wait_ge(s["yb_ready"], 1)
            dve.wait_ge(s["y_hi"], 2)
            dve.tensor_tensor(XL[:, 4:8, :], PROJ[:, 8:12, :], XH[:, 4:8, :].bitcast(F32),
                              ALU.subtract).then_inc(s["y_lo"], 1)
            dve.wait_ge(s["sig_ready"], 1)
            with dve.Fori(0, 2) as it:
                step.begin(it, 4)
                for j in range(4):
                    split_lo(C0["branch"] + j + 2, it, 4)
                    dve.wait_ge(chunk_done, at(C0["branch"] + j + 1, 4, it))
                    gates = PROJ[:, 12:28, :].rearrange("p (b m) t -> p b m t", b=2)[:, :, bass.ds(it * 4 + j, 1), :]
                    dve.tensor_tensor(TMPM[:, :, :].unsqueeze(2),
                                      ps[:, (U_BRANCH + j) % 4, :].rearrange("p (b o t) -> p b o t", b=2, o=1),
                                      gates, ALU.mult).then_inc(ring_evac, 1)
                    dve.wait_ge(ring_evac, at(U_BRANCH + j + 1, 4, it))
                    step.link(dve.tensor_tensor(MG[:, bass.ds(it * 4 + j, 1), :], TMPM[:, 0:1, :], TMPM[:, 1:2, :],
                                                ALU.add))
                step.end(2)
            dve.sem_inc(s["mg_ready"], 1)
            dve.wait_ge(s["m_hi"], 1)
            dve.tensor_tensor(ML[:, :, :], MG[:, :, :], MH[:, :, :].bitcast(F32), ALU.subtract).then_inc(s["m_lo"], 1)
            with dve.Fori(0, 2) as it:
                for j in range(4):
                    split_lo(C0["wout"] + j + 2, it, 4)
                    dve.wait_ge(chunk_done, at(C0["wout"] + j + 1, 4, it))
                    m = bass.ds(it * 4 + j, 1)
                    dve.tensor_tensor(H[:, m, :], ps[:, (U_WOUT + j) % 4, 0:T].unsqueeze(1), H[:, m, :],
                                      ALU.add).then_inc(ring_evac, 1)
            norm(1, H[:, :, :], TMP8[:, :, :], RMS[:, :], XH[:, :, :], XL[:, :, :],
                 lambda k, half: col("norm2", k))
            with dve.Fori(0, 3) as it:
                for j in range(4):
                    split_lo(C0["wq"] + j + 2, it, 4)
            split_lo(ADA - 2)
            split_lo(ADA - 1)

            with dve.Fori(0, PEER_HEADS) as it:
                step.begin(it, 11)
                dve.wait_ge(s["sc_ready"], it * 2 + 6)
                step.link(dve.tensor_copy(STG[:, :, :, :], SC[:, bass.ds(it * 2, 2), :, :]))
                units = [(side, tt) for side in range(2) for tt in range(TT)]
                step.apart()
                for sd, tt in units:
                    ins = dve.max(V16[:, sd, tt, 0:8], STG[:, sd, tt, :])
                step.link(ins)
                step.apart()
                for sd, tt in units:
                    dve.max_index(I16[:, sd, tt, 0:8], V16[:, sd, tt, 0:8], STG[:, sd, tt, :])
                    ins = dve.match_replace(STG2[:, sd, tt, :], V16[:, sd, tt, 0:8], STG[:, sd, tt, :], NEG)
                step.link(ins)
                step.apart()
                for sd, tt in units:
                    ins = dve.max(V16[:, sd, tt, 8:16], STG2[:, sd, tt, :])
                step.link(ins)
                step.apart()
                for sd, tt in units:
                    ins = dve.max_index(I16[:, sd, tt, 8:16], V16[:, sd, tt, 8:16], STG2[:, sd, tt, :])
                for tt in range(TT):
                    ins = dve.tensor_tensor(CAND[:, tt, :, :],
                                            V16[:, 0, tt, :].unsqueeze(2).to_broadcast([P, TOPK, TOPK]),
                                            V16[:, 1, tt, :].unsqueeze(1).to_broadcast([P, TOPK, TOPK]), ALU.add)
                step.link(ins)
                flat = [CAND[:, tt, :, :].rearrange("p a b -> p (a b)") for tt in range(TT)]
                flat2 = [CAND2[:, tt, :, :].rearrange("p a b -> p (a b)") for tt in range(TT)]
                h = bass.ds(it, 1)
                step.link(dve.tensor_copy(IF[:, :, :, h, :].rearrange("p s t o k -> p (s t) o k"),
                                          I16[:, :, :, :].rearrange("p s t (o k) -> p (s t) o k", o=1)))
                step.apart()
                for tt in range(TT):
                    ins = dve.max(CV[:, tt, 0:8], flat[tt])
                step.link(ins)
                step.apart()
                for tt in range(TT):
                    dve.max_index(CI[:, tt, 0:8], CV[:, tt, 0:8], flat[tt])
                    ins = dve.match_replace(flat2[tt], CV[:, tt, 0:8], flat[tt], NEG)
                step.link(ins)
                step.apart()
                for tt in range(TT):
                    ins = dve.max(CV[:, tt, 8:16], flat2[tt])
                step.link(ins)
                step.apart()
                for tt in range(TT):
                    ins = dve.max_index(CI[:, tt, 8:16], CV[:, tt, 8:16], flat2[tt])
                step.link(ins)
                dve.tensor_copy(VAL[:, :, h, :], CV[:, :, :].unsqueeze(2))
                step.link(dve.tensor_copy(CIU[:, :, h, :], CI[:, :, :].unsqueeze(2)))
                step.end(PEER_HEADS)
            full = [P, PEER_HEADS, TOPK]
            big = [P, PEER_HEADS, TOPK, TOPK]
            for tt in range(TT):
                ins = dve.tensor_copy(GSUM[:, tt, :].unsqueeze(2), VAL[:, tt, :, 0:1])
            step.link(ins)
            for tt in range(TT):
                ins = dve.tensor_tensor(VAL[:, tt, :, :], VAL[:, tt, :, :],
                                        GSUM[:, tt, :].unsqueeze(2).to_broadcast(full), ALU.subtract)
            ins.then_inc(s["vals_ready"], 1)
            dve.tensor_scalar(IAU[:, 0, :, :, :], CIU[:, :, :, :], 4, None, ALU.logical_shift_right)
            step.link(dve.tensor_scalar(IAU[:, 1, :, :, :], CIU[:, :, :, :], 15, None, ALU.bitwise_and))
            step.link(dve.tensor_copy(IAF[:, :, :, :, :], IAU[:, :, :, :, :]))
            dve.wait_ge(s["iota_ready"], 1)
            for sd in range(2):
                for tt in range(TT):
                    step.link(dve.tensor_tensor(EQ[:, :, :, :], IAF[:, sd, tt, :, :].unsqueeze(3).to_broadcast(big),
                                                IOTA16[:, :].unsqueeze(1).unsqueeze(1).to_broadcast(big), ALU.is_equal))
                    step.link(dve.tensor_tensor(EQ[:, :, :, :], EQ[:, :, :, :],
                                                IF[:, sd, tt, :, :].unsqueeze(2).to_broadcast(big), ALU.mult))
                    step.link(dve.tensor_reduce(SEL[:, sd, tt, :, :], EQ[:, :, :, :], AXX, ALU.add))
            dve.wait_ge(s["val_exp"], 1)
            step.link(dve.tensor_reduce(GSUM[:, :, :], VAL[:, :, :, :], AXX, ALU.add))
            step.link(dve.reciprocal(GSUM[:, :, :], GSUM[:, :, :]))
            for tt in range(TT):
                ins = dve.tensor_tensor(SEL[:, 2, tt, :, :], VAL[:, tt, :, :],
                                        GSUM[:, tt, :].unsqueeze(2).to_broadcast(full), ALU.mult)
            ins.then_inc(s["sel_ready"], 1)
            dve.wait_ge(s["lgd_ready"], 1)
            dve.scalar_tensor_tensor(LGD[:, 3, :], LGD[:, 0, :], 0.0, LGD[:, 2, :], ALU.min,
                                     ALU.subtract).then_inc(s["lgd_done"], 1)
            dve.wait_ge(chunk_done, ADA_END)
            bada = CL[:, COLS["bada"]:COLS["bada"] + MODB].unsqueeze(2).to_broadcast([P, MODB, 2])
            step.link(dve.tensor_tensor(MOD[:, :, :], ps[:, 6, 0:2 * MODB].rearrange("p (m c) -> p m c", c=2),
                                        bada, ALU.add))
            for n, name in enumerate(("ffn1", "mix", "ffn2")):
                sc = MOD[:, 24 * n + 8:24 * n + 16, :]
                dve.scalar_tensor_tensor(SCG[:, n, :, :], sc, 1.0,
                                         CL[:, COLS[name]:COLS[name] + KB].unsqueeze(2).to_broadcast([P, KB, 2]),
                                         ALU.add, ALU.mult)
            dve.tensor_scalar(GH[:, 0, :, :], MOD[:, 16:24, :], 0.5, None, ALU.mult)
            step.link(dve.tensor_scalar(GH[:, 1, :, :], MOD[:, 64:72, :], 0.5, None, ALU.mult))
            dve.wait_ge(s["slots_ready"], 1)
            dve.wait_ge(s["iota_ready"], 2)
            with dve.Fori(0, T // 16) as it:
                for q in range(4):
                    dve.wait_ge(s["onehot_used"], at(q + 1, 4, it))
                    for t in range(4):
                        tok = bass.ds(it * 16 + (4 * q + t), 1)
                        ins = dve.tensor_scalar(OI[:, q, t, :], IOTA[:, :], SLT[:, 0, tok], SLT[:, 2, tok],
                                                ALU.is_equal, ALU.mult)
                    ins.then_inc(s["oi_ready"], 1)

            PC = C0["peer"]

            def expert(e, it=None):
                q = e % 4
                dve.wait_ge(s["gelu_ready"], at(e + 1, 4, it))
                g = G[:, e:e + 1, :] if it is None else G[:, bass.ds(it * 4 + e, 1), :]
                dve.tensor_tensor(g, ps[:, q, 0:T].unsqueeze(1), g, ALU.mult).then_inc(s["gated_ready"], 1)

            def expert_lo(e, it=None):
                g = G[:, e:e + 1, :] if it is None else G[:, bass.ds(it * 4 + e, 1), :]
                dve.wait_ge(s["a_hi"], at(e + 1, 4, it))
                dve.tensor_tensor(AL[:, e % 2:e % 2 + 1, :], g, AH[:, e % 2:e % 2 + 1, :].bitcast(F32),
                                  ALU.subtract).then_inc(s["a_lo"], 1)

            for c in range(4):
                split_lo(PC + c)
            dve.wait_ge(s["g_ready"], T // 4 + 4)
            expert(0)
            expert_lo(0)

            def pair(e, it=None):
                split_lo(PC + 4 + 2 * e, it, 8)
                expert(e + 1, it)
                split_lo(PC + 5 + 2 * e, it, 8)
                expert_lo(e + 1, it)

            for e in range(2):
                pair(e)
            with dve.Fori(0, 31) as it:
                for e in range(2, 6):
                    pair(e, it)
            split_lo(PC + 256)
            expert(127)
            expert_lo(127)
            split_lo(PC + 257)
            dve.wait_ge(chunk_done, C0["up1"])
            dve.tensor_tensor(H[:, :, :], H[:, :, :], ps[:, 4:8, :].rearrange("p b (g t) -> p (b g) t", t=T),
                              ALU.add).then_inc(s["peer_added"], 1)
            norm(2, H[:, :, :], None, RMS5[:, 0:T], None, None, lambda k, half: col("final", k), dst=HX)

            def ffn(n, up, down, width, halves):
                with dve.Fori(0, FF // 2) as it:
                    for f in range(2):
                        c = up + 2 * f
                        split_lo(c + 2, it, 4)
                        split_lo(c + 3, it, 4)
                        dve.wait_ge(chunk_done, at(c + 2, 4, it))
                        dve.wait_ge(s["ffn_silu"], at(n * FF + f + 1, 2, it))
                        dve.tensor_tensor(HT[:, f, 0:width], TA[:, f, 0:width], ps[:, 2 * f + 1, 0:width],
                                          ALU.mult).then_inc(s["ffn_prod"], 1)
                        dve.wait_ge(s["ffn_hi"], at(n * FF + f + 1, 2, it))
                        dve.tensor_tensor(HIDL[:, bass.ds(it * 2 + f, 1), 0:width], HT[:, f, 0:width].unsqueeze(1),
                                          HIDH[:, bass.ds(it * 2 + f, 1), 0:width].bitcast(F32),
                                          ALU.subtract).then_inc(s["ffn_lo"], 1)
                with dve.Fori(0, 5) as it:
                    for j in range(4):
                        split_lo(down + j + 2, it, 4)
                for c in range(down + 22, min(down + 24, NCH)):
                    split_lo(c)
                dve.wait_ge(chunk_done, down + FF)
                for half in range(halves):
                    for m in range(KB):
                        src = ps[:, m, half * T:half * T + T] if width > T else ps[:, 4 + m // 2, (m % 2) * T:(m % 2) * T + T]
                        dst = HX[:, m, half * T:half * T + T]
                        ins = dve.scalar_tensor_tensor(dst, src, GH[:, n, m, half:half + 1], dst, ALU.mult, ALU.add)
                ins.then_inc(s["hx_ready"], 1)

            dve.wait_ge(s["ctx_landed"], 16)
            dve.sem_inc(s["ffn_prod"], 2)
            norm(3, HX, TMP16, RMS5[:, :], XH2_16, XL2_16,
                 lambda k, half: SCG[:, 0, k, half:half + 1], lambda k, half: MOD[:, k, half:half + 1])
            ffn(0, C0["up1"], C0["down1"], 2 * T, 2)
            norm(4, HX, TMP16, RMS5[:, :], XH2_16, XL2_16,
                 lambda k, half: SCG[:, 1, k, half:half + 1], lambda k, half: MOD[:, 24 + k, half:half + 1])

            HC = C0["heads"]
            dve.wait_ge(s["tables_landed"], 64)
            for name in ("p_ready", "on_ready", "yt_ready"):
                dve.sem_inc(s[name], 1)
            with dve.Fori(0, RH) as it:
                step.begin(it, 7)
                dve.wait_ge(s["decay_exp"], at(2, 2, it))
                dve.tensor_tensor(EF[:, 0:2, :], EF[:, 0:2, :], MASK[:, 0, :, :], ALU.mult)
                step.link(dve.tensor_tensor(EB[:, 0:2, :], EB[:, 0:2, :], MASK[:, 1, :, :], ALU.mult))
                step.link(dve.tensor_tensor(EF[:, :, :], EF[:, :, :], EB[:, :, :], ALU.add))
                for j in range(4):
                    split_lo(HC + j + 2, it, 12)
                dve.wait_ge(chunk_done, at(HC + 4, 12, it))
                cos, sin = ROPE[:, 0, :], ROPE[:, 1, :]
                for b, dst in ((0, QR), (2, KR)):
                    dve.tensor_tensor(RT[:, 0, :], ps[:, b, 0:T], cos, ALU.mult)
                    dve.tensor_tensor(RT[:, 1, :], ps[:, b + 1, 0:T], sin, ALU.mult)
                    dve.tensor_tensor(RT[:, 2, :], ps[:, b, 0:T], sin, ALU.mult)
                    step.link(dve.tensor_tensor(RT[:, 3, :], ps[:, b + 1, 0:T], cos, ALU.mult))
                    dve.tensor_tensor(dst[:, 0, 0:T], RT[:, 0, :], RT[:, 1, :], ALU.subtract)
                    ins = dve.tensor_tensor(dst[:, 1, 0:T], RT[:, 2, :], RT[:, 3, :], ALU.add)
                    if b == 0:
                        step.link(ins)
                ins.then_inc(s["qk_ready"], 1)
                for j in range(4, 8):
                    split_lo(HC + j + 2, it, 12)
                for j in range(8, 10):
                    split_lo(HC + j + 2, it, 12)
                dve.wait_ge(s["s_ready"], at(1, 1, it))
                dve.scalar_tensor_tensor(PT[:, :, :], ps[:, 0:2, :].rearrange("p b (g t) -> p (b g) t", t=T),
                                         1.0 / 16.0, EF[:, :, :], ALU.mult, ALU.mult).then_inc(s["p_ready"], 1)
                for j in range(10, 12):
                    split_lo(HC + j + 2, it, 12)
                dve.wait_ge(s["pv_ready"], at(2, 1, it))
                for tt in range(TT):
                    ins = dve.bn_stats(OST6[:, tt, :], ps[:, 4 + tt, :])
                step.link(ins)
                step.apart()
                for tt in range(TT):
                    ins = dve.bn_aggr(OMV[:, tt, :], OST6[:, tt, :])
                ins.then_inc(s["o_var"], 1)
                dve.wait_ge(s["o_std"], at(1, 1, it))
                step.link(dve.reciprocal(OMV[:, :, 1:2], OMV[:, :, 1:2]))
                for tt in range(TT):
                    ins = dve.tensor_scalar(ON[:, tt, :], ps[:, 4 + tt, :], OMV[:, tt, 0:1], OMV[:, tt, 1:2],
                                            ALU.subtract, ALU.mult)
                ins.then_inc(s["on_ready"], 1)
                dve.wait_ge(s["on_turned"], at(1, 1, it))
                dve.wait_ge(s["sg_ready"], at(2, 1, it))
                for v in range(4):
                    gain = CL[:, bass.ds(it * 4 + (COLS["gn"] + v), 1)]
                    ins = dve.scalar_tensor_tensor(YT[:, v, :], ps[:, 6 + v // 2, (v % 2) * T:(v % 2) * T + T],
                                                   gain, SG[:, v, :], ALU.mult, ALU.mult)
                ins.then_inc(s["yt_ready"], 1)
                dve.wait_ge(s["yr_hi"], at(1, 1, it))
                dve.tensor_tensor(YRL[:, bass.ds(it * 4, 4), :], YT[:, :, :],
                                  YRH[:, bass.ds(it * 4, 4), :].bitcast(F32), ALU.subtract).then_inc(s["yr_ready"], 1)
                step.end(RH)
            for c in range(8):
                split_lo(C0["four"] + c + 2)
            with dve.Fori(0, 4) as it:
                for j in range(4):
                    split_lo(C0["gates"] + j + 2, it, 4)
            dve.wait_ge(s["yf_hi"], 1)
            dve.tensor_tensor(YFL[:, :, :], ps[:, 0:4, :].rearrange("p b (g t) -> p (b g) t", t=T),
                              YFH[:, :, :].bitcast(F32), ALU.subtract).then_inc(s["yf_ready"], 1)
            with dve.Fori(0, 2) as it:
                step.begin(it, 4)
                for j in range(4):
                    for i in range(3):
                        split_lo(C0["proj"] + 3 * j + i + 2, it, 12)
                    dve.wait_ge(chunk_done, at(C0["proj"] + 3 * j + 3, 12, it))
                    gates = GS[:, :, :].rearrange("p (b m) t -> p b m t", b=2)[:, :, bass.ds(it * 4 + j, 1), :]
                    dve.tensor_tensor(TMP2[:, :, :].unsqueeze(2),
                                      ps[:, (U_PROJ + j) % 4, :].rearrange("p (b o t) -> p b o t", b=2, o=1),
                                      gates, ALU.mult).then_inc(ring_evac, 1)
                    dve.wait_ge(ring_evac, at(U_PROJ + j + 1, 4, it))
                    step.link(dve.tensor_tensor(MG2[:, bass.ds(it * 4 + j, 1), :], TMP2[:, 0:1, :], TMP2[:, 1:2, :],
                                                ALU.add))
                step.end(2)
            dve.sem_inc(s["mg2_ready"], 1)
            dve.wait_ge(s["m2_hi"], 1)
            dve.tensor_tensor(XL2_8, MG2[:, :, :], XH2_8.bitcast(F32), ALU.subtract).then_inc(s["m2_lo"], 1)
            with dve.Fori(0, 2) as it:
                for j in range(4):
                    split_lo(C0["wout2"] + j + 2, it, 4)
                    dve.wait_ge(chunk_done, at(C0["wout2"] + j + 1, 4, it))
                    m = bass.ds(it * 4 + j, 1)
                    dve.scalar_tensor_tensor(HX[:, m, 0:T], ps[:, (U_WOUT2 + j) % 4, 0:T].unsqueeze(1),
                                             MOD[:, bass.ds(it * 4 + (40 + j), 1), 0], HX[:, m, 0:T],
                                             ALU.mult, ALU.add).then_inc(ring_evac, 1)
            norm(5, HX, TMP16, RMS5[:, 0:T], XH2_8, XL2_8,
                 lambda k, half: SCG[:, 2, k, half:half + 1], lambda k, half: MOD[:, 48 + k, half:half + 1])
            ffn(1, C0["up2"], C0["down2"], T, 1)
            norm(6, HX, None, RMS5[:, 0:T], None, None, lambda k, half: col("last", k), dst=HX)

        @block.tensor
        def _(pe):
            def split_ready(c, it=None, n=0):
                pe.wait_ge(lo_ready, at(split_index(c) + 1, n, it))

            def bank_free(u, it=None, n=4):
                if u >= 4:
                    pe.wait_ge(ring_evac, at(u - 3, n, it))

            def product(dst, wh, wl, xh, xl, start, stop, check=True):
                pe.matmul(dst, wh, xh, start=start, stop=False, skip_group_check=not check)
                pe.matmul(dst, wh, xl, start=False, stop=False, skip_group_check=not check)
                return pe.matmul(dst, wl, xh, start=False, stop=stop, skip_group_check=not check)

            def feature_chunk(c, dst, xh, xl, it=None, n=0, k0=0, start=True, stop=True, inc=True):
                split_ready(c, it, n)
                slot = c % 4
                for k in range(KB):
                    w = slice(k * P, k * P + P)
                    ins = product(dst, WH[:, slot, w], WL[:, slot, w], xh[:, k0 + k, :], xl[:, k0 + k, :],
                                  start and k == 0, stop and k == KB - 1)
                ins.then_inc(chunk_done, 1)

            def token_chunk(c, part, bank, tiles, xh, xl, it=None, n=0):
                split_ready(c, it, n)
                slot = c % 4
                for kk in range(2):
                    k = 2 * part + kk
                    w = slice(kk * 512, kk * 512 + 512)
                    for tt in range(tiles):
                        t = slice(tt * P, tt * P + P)
                        dst = ps[:, bank + tt, :]
                        pe.matmul(dst, xh[:, k, t], WH[:, slot, w], start=(k == 0), stop=False)
                        pe.matmul(dst, xl[:, k, t], WH[:, slot, w], start=False, stop=False)
                        ins = pe.matmul(dst, xh[:, k, t], WL[:, slot, w], start=False, stop=(k == KB - 1))
                ins.then_inc(chunk_done, 1)

            def norm_sum(n, tmp, width):
                pe.wait_ge(s["norm_sq"], n + 1)
                for k in range(KB):
                    ins = pe.matmul(ps[:, 4, 0:width], ONES[:, :], tmp[:, k, 0:width], start=(k == 0), stop=(k == KB - 1))
                ins.then_inc(s["norm_sum"], 1)

            pe.wait_ge(s["pool_consts"], 5)
            norm_sum(0, TMP8, T)
            pe.wait_ge(s["norm_lo"], 1)
            feature_chunk(0, ps[:, 3, 0:T], XH, XL)
            for c in range(1, 13):
                n, part = divmod(c - 1, 4)
                if n == 2 and part == 0:
                    pe.wait_ge(s["tok_ready"], 1)
                token_chunk(c, part, 4 + 2 * (n % 2), TT, XH, XL)
            pe.wait_ge(ring_evac, U_FEAT)
            with pe.Fori(0, 7) as it:
                for j in range(4):
                    bank_free(U_FEAT + j, it)
                    feature_chunk(C0["feat"] + j, ps[:, (U_FEAT + j) % 4, 0:T], XH, XL, it, 4)
            pe.wait_ge(s["const_landed"], 16 * 12)
            pe.wait_ge(s["tok_ready"], 3)
            for tt in range(TT):
                ins = pe.matmul(ps[:, 4 + tt, :], ALR[0:17, tt * P:tt * P + P], WA2[:, :], start=True, stop=True)
            ins.then_inc(s["z_ready"], 1)
            pe.wait_ge(s["loga_ready"], 1)
            for tt in range(TT):
                pe.matmul(ps[:, 6 + tt, :], UM[:, :], LOGA[:, tt, :], start=True, stop=True)
            for tt in range(TT):
                for h in range(HEADS):
                    ins = pe.matmul(ps[:, 4, h * NCK + 2 * tt:h * NCK + 2 * tt + 2], LOGA[:, tt, h * P:h * P + P],
                                    BONES[:, :], start=True, stop=True)
            ins.then_inc(s["suffix_ready"], 1)
            pe.wait_ge(s["kdec_ready"], 1)
            pe.wait_ge(ring_evac, U_BRANCH)
            for c in range(NCK):
                rows = slice((c % 2) * CHUNK, (c % 2) * CHUNK + CHUNK)
                for h in range(HEADS):
                    hs = slice(h * P, h * P + P)
                    ins = pe.matmul(ps[:, c, hs], KT[rows, c // 2, hs], VT[rows, c // 2, hs], start=True, stop=True)
            ins.then_inc(s["kv_ready"], 1)
            pe.wait_ge(s["state_ready"], 1)
            pe.wait_ge(s["exs_ready"], 2)
            for h in range(HEADS):
                for c in range(NCK):
                    t0 = (h % 2) * T + c * CHUNK
                    ins = pe.matmul(ps[:, 4 + h // 2, t0:t0 + CHUNK], ST[:, c, h * P:h * P + P],
                                    PROJ[:, h, c * CHUNK:c * CHUNK + CHUNK], start=True, stop=True)
            ins.then_inc(s["o_ready"], 1)
            pe.wait_ge(s["vn_ready"], 1)
            for g in range(4):
                for nb in range(TT):
                    t0 = (g % 2) * T + nb * P
                    dst = ps[:, g // 2, t0:t0 + P]
                    pe.matmul(dst, SV[:, nb, g * P:g * P + P], WST[:, g, :], start=True, stop=False)
                    ins = pe.matmul(dst, ONES[0:1, :], BS[0:1, g * P:g * P + P], start=False, stop=True)
            ins.then_inc(s["mixed_ready"], 1)
            pe.wait_ge(s["og_sq"], 1)
            for b in range(2):
                ins = pe.matmul(ps[:, 6 + b, :], ONES[:, :], SQ2[:, 2 * b:2 * b + 2, :], start=True, stop=True)
            ins.then_inc(s["og_sum"], 1)
            pe.wait_ge(s["y_lo"], 1)
            with pe.Fori(0, 2) as it:
                for j in range(4):
                    c = C0["branch"] + j
                    bank_free(U_BRANCH + j, it)
                    split_ready(c, it, 4)
                    for k in range(KB):
                        w = slice(k * P, k * P + P)
                        dst = ps[:, (U_BRANCH + j) % 4, (k // 4) * T:(k // 4) * T + T]
                        ins = product(dst, WH[:, c % 4, w], WL[:, c % 4, w], XH[:, k, :], XL[:, k, :],
                                      k % 4 == 0, k % 4 == 3)
                    ins.then_inc(chunk_done, 1)
            pe.wait_ge(s["m_lo"], 1)
            with pe.Fori(0, 2) as it:
                for j in range(4):
                    bank_free(U_WOUT + j, it)
                    feature_chunk(C0["wout"] + j, ps[:, (U_WOUT + j) % 4, 0:T], MH, ML, it, 4)
            norm_sum(1, TMP8, T)
            pe.wait_ge(s["norm_lo"], 2)

            def scores(j, it):
                pe.wait_ge(ring_evac, at(U_WQ + j + 1, 4, it))
                pe.wait_ge(s["sc_ready"], at(j + 1, 4, it))
                for tt in range(TT):
                    ins = pe.matmul(ps[:, 4 + j, tt * P:tt * P + P], QT[:, j, tt * P:tt * P + P], K12T[:, j % 2, :],
                                    start=True, stop=True)
                ins.then_inc(s["scores_ready"], 1)

            pe.sem_inc(s["scores_ready"], 4)
            with pe.Fori(0, 4) as it:
                for j in range(4):
                    bank_free(U_WQ + j, it)
                    feature_chunk(C0["wq"] + j, ps[:, (U_WQ + j) % 4, 0:T], XH, XL, it, 4)
                    if j:
                        scores(j - 1, it)
                scores(3, it)
            pe.wait_ge(s["cs_ready"], 1)
            pe.wait_ge(s["sc_ready"], 16 + 4)
            with pe.Fori(0, MODB // 4) as it:
                for j in range(4):
                    c = ADA + j
                    pe.wait_ge(landed[c % 4], at(16 * (c // 4 + 1), 16, it))
                    for k in range(KB):
                        ins = pe.matmul(ps[:, 6, bass.ds(it * 8 + 2 * j, 2)], RAW[:, c % 4, k * P:k * P + P],
                                        CS[:, k, :], start=(k == 0), stop=(k == KB - 1))
                    ins.then_inc(chunk_done, 1)
            pe.wait_ge(s["sel_ready"], 1)
            for n in range(3):
                for tt in range(TT):
                    ins = pe.transpose(ps[:, 4 + n // 2, (n % 2) * T + tt * P:(n % 2) * T + tt * P + P],
                                       SEL[:, n, tt, :, :].rearrange("p h k -> p (h k)"), IDENT[:, :])
            ins.then_inc(s["slots_turned"], 1)
            pe.sem_inc(s["onehot_used"], 4)
            with pe.Fori(0, T // 16) as it:
                for q in range(4):
                    pe.wait_ge(s["oj_ready"], at(q + 1, 4, it))
                    pe.wait_ge(s["oi_ready"], at(q + 1, 4, it))
                    pe.wait_ge(s["g_ready"], at(q + 1, 4, it))
                    for t in range(4):
                        ins = pe.matmul(ps[:, q, t * P:t * P + P], OJ[:, q, t, :], OI[:, q, t, :], start=True, stop=True)
                    ins.then_inc(s["onehot_used"], 1)

            PC = C0["peer"]

            def up(e, c, it=None):
                feature_chunk(c, ps[:, e % 4, 0:T], XH, XL, it, 8)

            def down(e, c, it=None, last=False):
                split_ready(c, it, 8)
                pe.wait_ge(s["a_lo"], at(e + 1, 4, it))
                for m in range(KB):
                    w = slice(m * P, m * P + P)
                    ins = product(ps[:, 4 + m // 2, (m % 2) * T:(m % 2) * T + T], WH[:, c % 4, w], WL[:, c % 4, w],
                                  AH[:, e % 2, :], AL[:, e % 2, :], False, last, check=False)
                ins.then_inc(chunk_done, 1)

            pe.wait_ge(s["g_ready"], T // 4 + 4)
            for b in range(4):
                for i in range(4):
                    pe.matmul(ps[:, 4 + b, i * P:i * P + P], ZR[0:1, :], ONES[0:1, :], start=(i == 0), stop=False,
                              skip_group_check=True)
            up(0, PC)
            up(1, PC + 1)

            def pair(e, it=None):
                if e >= 2:
                    pe.wait_ge(s["gated_ready"], at(e - 1, 4, it))
                up(e + 2, PC + 2 + 2 * e, it)
                down(e, PC + 3 + 2 * e, it)

            for e in range(2):
                pair(e)
            with pe.Fori(0, 31) as it:
                for e in range(2, 6):
                    pair(e, it)
            down(126, PC + 254)
            down(127, PC + 255, last=True)
            pe.wait_ge(s["peer_added"], 1)
            norm_sum(2, TMP16, T)

            def ffn(n, upc, downc, width, xh, xl):
                with pe.Fori(0, FF // 2) as it:
                    for j in range(4):
                        pe.wait_ge(s["ffn_prod"], at(n * FF + j // 2 + 1, 2, it))
                        feature_chunk(upc + j, ps[:, j, 0:width], xh, xl, it, 4)
                pe.wait_ge(s["ffn_lo"], FF * (n + 1))

                def hidden(c, k, it=None, step_=4, first=False, last=False):
                    split_ready(c, it, step_)
                    kk = slice(k, k + 1) if it is None else bass.ds(it * 4 + k, 1)
                    for m in range(KB):
                        w = slice(m * P, m * P + P)
                        if width > T:
                            dst, opens = ps[:, m, :].unsqueeze(1), True
                        else:
                            dst, opens = ps[:, 4 + m // 2, (m % 2) * T:(m % 2) * T + T].unsqueeze(1), m % 2 == 0
                        ins = product(dst, WH[:, c % 4, w], WL[:, c % 4, w], HIDH[:, kk, 0:width], HIDL[:, kk, 0:width],
                                      first and opens, last, check=False)
                    ins.then_inc(chunk_done, 1)

                hidden(downc, 0, first=True)
                with pe.Fori(0, 5) as it:
                    for j in range(4):
                        hidden(downc + 1 + j, 1 + j, it)
                hidden(downc + 21, 21, last=True)

            norm_sum(3, TMP16, 2 * T)
            pe.wait_ge(s["norm_lo"], 3)
            ffn(0, C0["up1"], C0["down1"], 2 * T, XH2_16, XL2_16)
            pe.wait_ge(s["hx_ready"], 1)
            norm_sum(4, TMP16, 2 * T)
            pe.wait_ge(s["norm_lo"], 4)
            HC = C0["heads"]
            pe.sem_inc(s["pv_ready"], 1)
            with pe.Fori(0, RH) as it:
                pe.wait_ge(s["p_ready"], it + 1)
                pe.wait_ge(s["sg_ready"], it + 1)
                for j in range(2):
                    feature_chunk(HC + j, ps[:, j, 0:T], XH2_16[:, :, 0:T], XL2_16[:, :, 0:T], it, 12)
                for j in range(2, 4):
                    feature_chunk(HC + j, ps[:, j, :], XH2_16, XL2_16, it, 12)
                pe.wait_ge(s["on_ready"], it + 1)
                pe.wait_ge(s["yt_ready"], it + 1)
                for j in range(4):
                    token_chunk(HC + 4 + j, j, 4, 4, XH2_16, XL2_16, it, 12)
                pe.wait_ge(s["qk_ready"], at(1, 1, it))
                pe.wait_ge(s["kctx_ready"], at(1, 1, it))
                for jt in range(4):
                    for d in range(2):
                        ins = pe.matmul(ps[:, jt // 2, (jt % 2) * T:(jt % 2) * T + T], KR[:, d, jt * P:jt * P + P],
                                        QR[:, d, :], start=(d == 0), stop=(d == 1))
                ins.then_inc(s["s_ready"], 1)
                for j in range(4):
                    feature_chunk(HC + 8 + j, ps[:, 2 + j // 2, (j % 2) * T:(j % 2) * T + T],
                                  XH2_16[:, :, 0:T], XL2_16[:, :, 0:T], it, 12)
                pe.wait_ge(s["p_ready"], at(2, 1, it))
                pe.wait_ge(s["v_ready"], at(1, 1, it))
                for tt in range(TT):
                    for jt in range(4):
                        ins = pe.matmul(ps[:, 4 + tt, :], PT[:, jt, tt * P:tt * P + P], VR[:, jt, :],
                                        start=(jt == 0), stop=(jt == 3))
                ins.then_inc(s["pv_ready"], 1)
                pe.wait_ge(s["on_ready"], at(2, 1, it))
                for v in range(4):
                    for tt in range(TT):
                        t0 = (v % 2) * T + tt * P
                        ins = pe.transpose(ps[:, 6 + v // 2, t0:t0 + P], ON[:, tt, v * P:v * P + P], IDENT2[:, :])
                ins.then_inc(s["on_turned"], 1)
            pe.wait_ge(s["on_ready"], RH + 1)
            pe.wait_ge(s["yt_ready"], RH + 1)
            for c in range(8):
                token_chunk(C0["four"] + c, c % 4, 4 + 2 * (c // 4), TT, XH2_16, XL2_16)
            pe.wait_ge(s["sg_ready"], RH + 1)
            with pe.Fori(0, 4) as it:
                for j in range(4):
                    bank_free(U_GATES + j, it)
                    feature_chunk(C0["gates"] + j, ps[:, (U_GATES + j) % 4, 0:T], XH2_16[:, :, 0:T], XL2_16[:, :, 0:T], it, 4)
            pe.wait_ge(s["ft_ready"], 2)
            pe.wait_ge(s["tables_landed"], 96)
            for n in range(KB):
                if n >= 4:
                    pe.wait_ge(s["ab_ready"], n - 3)
                for tt in range(TT):
                    ins = pe.matmul(ps[:, 4 + n % 4, :], FT[:, tt, n * P:n * P + P], DFTL[:, tt, :],
                                    start=(tt == 0), stop=(tt == TT - 1))
                ins.then_inc(s["dft_tok"], 1)
            pe.wait_ge(s["ab_ready"], KB)
            pe.wait_ge(ring_evac, U_PROJ)
            for n in range(KB):
                dst = ps[:, n // 2, (n % 2) * T:(n % 2) * T + T]
                for cb in range(2):
                    for part in range(2):
                        ins = pe.matmul(dst, DFTD[:, cb, part, (n % 2) * P:(n % 2) * P + P],
                                        AB[:, 2 * (n // 2) + cb, part * T:part * T + T],
                                        start=(cb == 0 and part == 0), stop=(cb == 1 and part == 1))
            ins.then_inc(s["dft_feat"], 1)
            pe.wait_ge(s["yf_ready"], 1)
            pe.wait_ge(s["yr_ready"], RH)
            with pe.Fori(0, 2) as it:
                for j in range(4):
                    c, b = C0["proj"] + 3 * j, (U_PROJ + j) % 4
                    bank_free(U_PROJ + j, it)
                    feature_chunk(c, ps[:, b, 0:T], YRH, YRL, it, 12, stop=False)
                    feature_chunk(c + 1, ps[:, b, 0:T], YRH, YRL, it, 12, k0=KB, start=False)
                    feature_chunk(c + 2, ps[:, b, T:2 * T], YFH, YFL, it, 12)
            pe.wait_ge(s["m2_lo"], 1)
            with pe.Fori(0, 2) as it:
                for j in range(4):
                    bank_free(U_WOUT2 + j, it)
                    feature_chunk(C0["wout2"] + j, ps[:, (U_WOUT2 + j) % 4, 0:T], XH2_8, XL2_8, it, 4)
            norm_sum(5, TMP16, T)
            pe.wait_ge(s["norm_lo"], 5)
            ffn(1, C0["up2"], C0["down2"], T, XH2_8, XL2_8)
            norm_sum(6, TMP16, T)


def lay_out(x):
    import numpy as np

    def features(w):
        k, n = w.shape
        return w.reshape(k // P, P, n // P, P).transpose(2, 1, 0, 3).reshape(n // P, P, -1)

    def tokens(w):
        return w.reshape(4, 2, P, 512).transpose(0, 2, 1, 3).reshape(4, P, 1024)

    def vec(v):
        return v.reshape(-1, P).T

    w = x["w_in"][0]
    q, k, v, r, alr, su, sv, ga, gb = np.split(w, [512, 1024, 1536, 2048, 2064, 2576, 3088, 4112], axis=1)
    parts = [features(np.concatenate([alr, np.zeros((D, P - 16), alr.dtype)], axis=1))]
    parts += [tokens(k), tokens(v), tokens(sv)]
    parts += [features(np.concatenate([q, r, su, ga, gb], axis=1))]
    parts += [features(np.concatenate([x["w_branch_a"][0], x["w_branch_b"][0]], axis=0)), features(x["w_out"][0])]
    parts += [features(x["peer_wq"][0]), features(x["w_ada_2"][0])]
    up = features(x["peer_u"][0].T)
    down = x["peer_v"][0].reshape(P, P, D)
    order = [up[0:1], up[1:2]]
    for e in range(P):
        if e + 2 < P:
            order.append(up[e + 2:e + 3])
        order.append(down[e:e + 1])
    parts += order

    def ffn(w13, w2):
        f = features(w13).reshape(2, FF, P, 1024).transpose(1, 0, 2, 3).reshape(2 * FF, P, 1024)
        return [f, w2.reshape(FF, P, D)]

    parts += ffn(x["w13_ffn1_2"][0], x["w2_ffn1_2"][0])
    w = x["w_in_2"][0]
    for h in range(RH):
        for c0 in (256 * h, 1024 + 256 * h):
            parts += [features(w[:, c0:c0 + 256:2]), features(w[:, c0 + 1:c0 + 256:2])]
        parts += [tokens(w[:, 2048 + 512 * h:2560 + 512 * h]), features(w[:, 4096 + 512 * h:4608 + 512 * h])]
    parts += [tokens(w[:, 6144:6656]), tokens(w[:, 6656:7168]), features(w[:, 7168:9216])]
    ret, four = features(x["p_ret_2"][0]), features(x["p_four_2"][0])
    for m in range(KB):
        parts += [ret[m:m + 1, :, 0:1024], ret[m:m + 1, :, 1024:2048], four[m:m + 1]]
    parts += [features(x["w_out_2"][0])]
    parts += ffn(x["w13_ffn2_2"][0], x["w2_ffn2_2"][0])
    stream = np.concatenate(parts, axis=0)
    assert stream.shape == (NCH, P, 1024)

    def acts(v):
        return v.T.reshape(KB, P, T).transpose(1, 0, 2)

    one = np.float64(1)
    i, p = np.arange(T)[None, None, :], np.arange(P)[:, None, None]
    j = p + P * np.arange(2)[None, :, None]
    fwd = np.concatenate([np.maximum(i - j, 0), T + i - j], axis=1)
    bwd = np.concatenate([np.maximum(j - i, 0), T - i + j], axis=1)
    inv = np.float32(10000.0) ** (-np.arange(64, dtype=np.float32) / np.float32(64))
    row, column = (np.arange(T) // 64).astype(np.float32), (np.arange(T) % 64).astype(np.float32)
    ang = np.concatenate([inv[:, None] * row[None], inv[:, None] * column[None]], axis=0).astype(np.float64)
    turn = 2 * np.pi * one / T
    lt = turn * ((np.arange(T)[:, None] * np.arange(T)[None, :]) % T)
    cos, sin = (np.cos(lt) / 16).reshape(2, P, T), (np.sin(lt) / 16).reshape(2, P, T)
    sidx = np.arange(P)
    same = sidx[:, None] // CHUNK == sidx[None, :] // CHUNK
    f = np.float32
    out = {
        "wstream": stream,
        "xT": acts(x["x"][0]), "ctxT": acts(x["ctx_2"][0]),
        "cols": np.concatenate([vec(x[n].reshape(-1)) for n in (
            "norm1_g", "norm2_g", "final_g", "gla_norm_g", "norm_ffn1_2", "norm_mix_2", "norm_ffn2_2",
            "norm_final_2", "ret_gn_w_2", "b_ada_2")], axis=1),
        "wa2b": np.concatenate([x["w_gate_up"][0], x["b_gate"]], axis=0),
        "wsT": x["sgu_w"][0].transpose(2, 0, 1), "bs": x["sgu_b"].reshape(1, 512),
        "lng": np.repeat(x["sgu_ln_g"], P, axis=0), "lnb": np.repeat(x["sgu_ln_b"], P, axis=0),
        "k12T": np.stack([x["peer_k1"][0].T, x["peer_k2"][0].T], axis=1),
        "cT": np.stack([vec(x["c_2"][0]), vec(x["c_ctx_2"])], axis=2),
        "decays": np.repeat(np.concatenate([x["decay_fwd_2"], x["decay_bwd_2"]], axis=1), P, axis=0),
        "umat": ((sidx[:, None] > sidx[None, :]) & same).astype(f) / f(TAU),
        "bones": (sidx[:, None] // CHUNK == np.arange(2)[None, :]).astype(f) / f(TAU),
        "ident": np.eye(P, dtype=f),
        "dist": np.stack([fwd, bwd], axis=1).astype(f),
        "mask": np.stack([i >= j, j >= i], axis=1).astype(f),
        "rope": np.stack([np.cos(ang), np.sin(ang)], axis=1).astype(f),
        "dftl": np.concatenate([cos, sin], axis=2).transpose(1, 0, 2).astype(f),
        "dftd": np.stack([cos, -sin], axis=2).transpose(1, 0, 2, 3).astype(f),
    }
    return {n: np.ascontiguousarray(v) for n, v in out.items()}


def kernel(**inputs):
    import numpy as _np
    import concourse.bacc as _bacc
    from concourse.bass_utils import run_bass_kernel_spmd as _run

    laid = lay_out({n: _np.asarray(v) for n, v in inputs.items()})
    nc = _bacc.Bacc("TRN2", target_bir_lowering=False, num_devices=1)
    arrays, args = {}, {}
    for n, v in laid.items():
        arrays[f"in_{n}"] = v
        args[n] = nc.dram_tensor(f"in_{n}", v.shape, mybir.dt.from_np(v.dtype), kind="ExternalInput").ap()
    out = nc.dram_tensor("out_0", (P, KB, T), F32, kind="ExternalOutput").ap()
    build(nc, args, out)
    r = _run(nc, [arrays], core_ids=[0])
    got = r.results[0]["out_0"]
    return got.transpose(2, 1, 0).reshape(1, T, D)
```

```python
import concourse.bass as bass
from concourse import mybir
from contextlib import ExitStack

F32 = mybir.dt.float32
F32R = mybir.dt.float32r
U32 = mybir.dt.uint32
ACT = mybir.ActivationFunctionType
ALU = mybir.AluOpType
AXX = mybir.AxisListType.X

P = 128
D = 1024
KB = D // P
T = 256
TT = T // P
EPS = 1e-6
HEADS = 4
CHUNK = 64
NCK = T // CHUNK
TAU = 16.0
PEER_HEADS, TOPK, NKEYS = 8, 16, 128
SLOTS = PEER_HEADS * TOPK
NEG = -3.0e38
FF = 2816 // P
RH, RV = 4, 512
N_MOD = 9
MODB = N_MOD * KB
ADA1 = 10
ADA2 = MODB // 4 - ADA1

ORDER = [
    ("alr", 1),
    ("tok", 12),
    ("feat", 28),
    ("branch", 8),
    ("wout", 8),
    ("wq", 16),
    ("ada", MODB),
    ("peer", 256),
    ("up1", 2 * FF), ("down1", FF),
    ("heads", 12 * RH),
    ("four", 8),
    ("gates", 16),
    ("proj", 24),
    ("wout2", 8),
    ("up2", 2 * FF), ("down2", FF),
]
C0, _n = {}, 0
for _name, _count in ORDER:
    C0[_name] = _n
    _n += _count
NCH = _n

COLS = {}
_n = 0
for _name, _count in [("norm1", 8), ("norm2", 8), ("final", 8), ("gla", 4), ("ffn1", 8), ("mix", 8),
                      ("ffn2", 8), ("last", 8), ("gn", 16), ("bada", MODB)]:
    COLS[_name] = _n
    _n += _count
NCOLS = _n


SPLIT_NORM = {0: 0, 1: 1, 3: 2, 4: 3, 5: 4}
NORM_BANK = (4, 4, 4, 4, 0, 4, 0)


def at(first, step, it):
    return first if it is None else it * step + first


class Tally:

    def __init__(self, eng, sem, spacer=None):
        self.eng, self.sem, self.spacer, self.n, self.it, self.per = eng, sem, spacer, 0, None, 0

    def link(self, ins):
        self.n += 1
        ins.then_inc(self.sem, 1)
        self.eng.wait_ge(self.sem, at(self.n, self.per, self.it))

    def apart(self):
        self.eng.sem_inc(self.spacer, 1)

    def begin(self, it, per):
        self.it, self.per, self.start = it, per, self.n

    def end(self, rounds):
        assert self.n - self.start == self.per, (self.n - self.start, self.per)
        self.n = self.start + self.per * rounds
        self.it, self.per = None, 0


class Sems(dict):

    def __init__(self, nc, ctx):
        self.nc, self.ctx = nc, ctx

    def __missing__(self, name):
        self[name] = self.ctx.enter_context(self.nc.semaphore(name))
        return self[name]


def build(nc, a, out):
    ctx = ExitStack()
    with ctx:
        s = Sems(nc, ctx)
        base = 16512
        place = [0]

        def sb(name, shape, offset=None, dt=F32):
            size = 4
            for d in shape[1:]:
                size *= d
            if offset is None:
                offset = place[0]
            place[0] = offset + (size + 31) // 32 * 32
            return nc.alloc_sbuf_tensor_at(name, shape, dt, offset=base + offset)

        RAW = sb("RAW", [P, 4, 1024], 0)
        WH = sb("WH", [P, 4, 1024], dt=F32R)
        WL = sb("WL", [P, 4, 1024], dt=F32R)
        H = sb("H", [P, KB, T])
        XH = sb("XH", [P, KB, T], dt=F32R)
        XL = sb("XL", [P, KB, T], dt=F32R)
        AHP = place[0]
        AH = sb("AH", [P, 2, T], dt=F32R)
        AL = sb("AL", [P, 2, T], dt=F32R)
        REG = place[0]
        G = sb("G", [P, NKEYS, T])
        CL = sb("CL", [P, NCOLS])
        MOD = sb("MOD", [P, MODB, 2])
        SCG = sb("SCG", [P, 3, KB, 2])
        GH = sb("GH", [P, 2, KB, 2])
        ONES = sb("ONES", [P, P])
        ZR = sb("ZR", [P, P])
        EPSC = sb("EPSC", [P, 1])
        LGD = sb("LGD", [P, 4, 8])
        CS = sb("CS", [P, KB, 2])
        ID2 = sb("ID2", [2, 2])
        assert base + place[0] <= nc.sbuf_usable_end

        PROJ = sb("PROJ", [P, 28, T], REG)
        KT = sb("KT", [P, TT, 512])
        VT = sb("VT", [P, TT, 512])
        SV = sb("SV", [P, TT, 512])
        ALR = sb("ALR", [32, T])
        WA2 = sb("WA2", [17, 512])
        LG1 = sb("LG1", [P, TT, 512])
        LOGA = sb("LOGA", [P, TT, 512])
        EXS = sb("EXS", [P, TT, 512])
        ST = sb("ST", [P, NCK, HEADS * P])
        DEC = sb("DEC", [P, HEADS, NCK])
        OG = sb("OG", [P, HEADS, T])
        RMS2 = sb("RMS2", [P, HEADS, T])
        SQ2 = sb("SQ2", [P, HEADS, T])
        TMP8 = sb("TMP8", [P, KB, T])
        RMS = sb("RMS", [P, T])
        UM = sb("UM", [P, P])
        BONES = sb("BONES", [P, 2])
        WST = sb("WST", [P, 4, P])
        BS = sb("BS", [1, 512])
        LNG = sb("LNG", [P, 512])
        LNB = sb("LNB", [P, 512])
        ST6 = sb("ST6", [P, TT, 6])
        MV = sb("MV", [P, TT, 2])
        TMPM = sb("TMPM", [P, 2, T])
        MG = sb("MG", [P, KB, T])
        KEEP = REG + 131072 - 8192
        assert place[0] <= KEEP
        IDENT = sb("IDENT", [P, P], KEEP)
        K12T = sb("K12T", [P, 2, P])
        QT = sb("QT", [P, 4, T])
        assert place[0] <= REG + 131072
        MH = sb("MH", [P, KB, T], REG + 28672, dt=F32R)
        ML = sb("ML", [P, KB, T], dt=F32R)
        SC = sb("SC", [P, 16, TT, NKEYS], REG)
        STG = sb("STG", [P, 2, TT, NKEYS])
        STG2 = sb("STG2", [P, 2, TT, NKEYS])
        V16 = sb("V16", [P, 2, TT, TOPK])
        I16 = sb("I16", [P, 2, TT, TOPK], dt=U32)
        CAND = sb("CAND", [P, TT, TOPK, TOPK], REG + 28672)
        CAND2 = sb("CAND2", [P, TT, TOPK, TOPK])
        CV = sb("CV", [P, TT, TOPK])
        CI = sb("CI", [P, TT, TOPK], dt=U32)
        VAL = sb("VAL", [P, TT, PEER_HEADS, TOPK])
        CIU = sb("CIU", [P, TT, PEER_HEADS, TOPK], dt=U32)
        IAU = sb("IAU", [P, 2, TT, PEER_HEADS, TOPK], dt=U32)
        IAF = sb("IAF", [P, 2, TT, PEER_HEADS, TOPK])
        IF = sb("IF", [P, 2, TT, PEER_HEADS, TOPK])
        EQ = sb("EQ", [P, PEER_HEADS, TOPK, TOPK])
        SEL = sb("SEL", [P, 3, TT, PEER_HEADS, TOPK])
        GSUM = sb("GSUM", [P, TT, PEER_HEADS])
        IOTA16 = sb("IOTA16", [P, TOPK])
        assert place[0] <= REG + 65536
        MROW = sb("MROW", [2, ADA1 * 512], REG + 57344)
        assert place[0] <= KEEP
        OJ = sb("OJ", [P, 2, 8, P], 16384)
        OI = sb("OI", [P, 2, 8, P])
        MROW2 = sb("MROW2", [2, ADA2 * 512])
        assert place[0] <= 49152
        SLT = sb("SLT", [P, 3, T], AHP)
        IOTA = sb("IOTA", [P, P])
        assert place[0] <= REG

        HX = sb("HX", [P, KB, 2 * T], 57344)
        XH2 = sb("XH2", [P, KB * 2 * T], REG, dt=F32R)
        XL2 = sb("XL2", [P, KB * 2 * T], dt=F32R)
        R2 = place[0]
        HIDH = sb("HIDH", [P, FF, 2 * T], R2, dt=F32R)
        HIDL = sb("HIDL", [P, FF, 2 * T], dt=F32R)
        TA = sb("TA", [P, 2, 2 * T])
        HT = sb("HT", [P, 2, 2 * T])
        TMP16 = sb("TMP16", [P, KB, 2 * T], R2)
        RMS5 = sb("RMS5", [P, 2 * T])
        YRH = sb("YRH", [P, 16, T], R2, dt=F32R)
        YRL = sb("YRL", [P, 16, T], dt=F32R)
        GS = sb("GS", [P, 16, T])
        R3 = place[0]
        QR = sb("QR", [P, 2, T])
        KR = sb("KR", [P, 2, 2 * T])
        VR = sb("VR", [P, 4, RV])
        SG = sb("SG", [P, 4, T])
        EF = sb("EF", [P, 4, T])
        EB = sb("EB", [P, 4, T])
        PT = sb("PT", [P, 4, T])
        ON = sb("ON", [P, TT, RV])
        YT = sb("YT", [P, 4, T])
        RT = sb("RT", [P, 4, T])
        MASK = sb("MASK", [P, 2, 2, T])
        ROPE = sb("ROPE", [P, 2, T])
        assert place[0] <= REG + 131072
        FT = sb("FT", [P, TT, D], R3)
        AB = sb("AB", [P, KB, 2 * T])
        DFTL = sb("DFTL", [P, TT, 2 * T])
        DFTD = sb("DFTD", [P, 2, 2, T])
        YFH = sb("YFH", [P, KB, T], dt=F32R)
        YFL = sb("YFL", [P, KB, T], dt=F32R)
        assert place[0] <= REG + 131072
        MG2 = sb("MG2", [P, KB, T], R3)
        TMP2 = sb("TMP2", [P, 2, T])
        DIST = sb("DIST", [P, 2, 4, T], 49152)
        IDENT2 = sb("IDENT2", [P, P], 73728)
        OST6 = sb("OST6", [P, TT, 6])
        OMV = sb("OMV", [P, TT, 2])
        assert place[0] <= REG

        ps = ctx.enter_context(nc.psum_tensor("ps", [P, 8, 512], F32))

        def col(name, k):
            return CL[:, COLS[name] + k:COLS[name] + k + 1]

        XH2_8 = XH2[:, 0:KB * T].rearrange("p (k t) -> p k t", k=KB)
        XL2_8 = XL2[:, 0:KB * T].rearrange("p (k t) -> p k t", k=KB)
        XH2_16 = XH2[:, :].rearrange("p (k t) -> p k t", k=KB)
        XL2_16 = XL2[:, :].rearrange("p (k t) -> p k t", k=KB)

        landed = [s[f"raw_landed{j}"] for j in range(4)]
        hi_ready = s["hi_ready"]
        lo_ready = s["lo_ready"]
        chunk_done = s["chunk_done"]
        ring_evac = s["ring_evac"]
        ADA, ADA_END = C0["ada"], C0["ada"] + MODB

        def split_index(c):
            return c if c < ADA else c - MODB

        U_ALR, U_FEAT = 3, 4
        U_BRANCH = U_FEAT + 28
        U_WOUT = U_BRANCH + 8
        U_WQ = U_WOUT + 8
        U_GATES = U_WQ + 16
        U_PROJ = U_GATES + 16
        U_WOUT2 = U_PROJ + 8
        U_END = U_WOUT2 + 8

        block = ctx.enter_context(nc.Block())

        @block.sync
        def _(sp):
            def load(slot, c, count=0):
                sp.dma_start(RAW[:, slot, :], a["wstream"][c]).then_inc(landed[slot], 16)

            sp.dma_start(H[:, :, :], a["xT"]).then_inc(s["x_landed"], 16)
            sp.dma_start(CL[:, :], a["cols"]).then_inc(s["cols_landed"], 16)
            for c in range(4):
                load(c, c)
            for dst, name in ((WA2[:, :], "wa2b"), (UM[:, :], "umat"),
                              (BONES[:, :], "bones"), (WST[:, :, :], "wsT"), (BS[:, :], "bs"),
                              (LNG[:, :], "lng"), (LNB[:, :], "lnb"), (IDENT[:, :], "ident"),
                              (K12T[:, :, :], "k12T"), (CS[:, :, :], "cT"), (LGD[:, 0, :], "decays")):
                sp.dma_start(dst, a[name]).then_inc(s["const_landed"], 16)
            with sp.Fori(0, 18) as it:
                for j in range(4):
                    sp.wait_ge(lo_ready, at(j + 1, 4, it))
                    load(j, it * 4 + (j + 4))
            sp.wait_ge(lo_ready, 73)
            load(0, 76)
            with sp.Fori(0, MODB // 4) as it:
                for j in range(4):
                    sp.wait_ge(chunk_done, at(74 + j, 4, it))
                    load((77 + j) % 4, it * 4 + (77 + j))
            with sp.Fori(0, (NCH - 149) // 4) as it:
                for j in range(4):
                    sp.wait_ge(lo_ready, at(149 + j - 3 - MODB, 4, it))
                    load((149 + j) % 4, it * 4 + (149 + j))
            sp.wait_ge(s["norm_out"], 7 * KB)
            sp.dma_start(out, HX[:, :, 0:T]).then_inc(s["out_written"], 16)
            sp.wait_ge(s["out_written"], 16)

        @block.gpsimd
        def _(pool):
            for n, (dst, value) in enumerate(((ONES, 1.0), (ZR, 0.0), (EPSC, EPS), (ALR, 1.0))):
                pool.memset(dst[:, :], value).then_inc(s["pool_consts"], 1)
                pool.wait_ge(s["pool_consts"], n + 1)
            pool.wait_ge(s["const_landed"], 16 * 11)
            pool.memset(WST[64:128, :, 0:64], 0.0).then_inc(s["pool_consts"], 1)
            pool.wait_ge(ring_evac, U_WOUT)
            pool.iota(IOTA16[:, :], [[1, TOPK]], 0, 0, allow_small_or_imprecise_dtypes=True).then_inc(s["iota_ready"], 1)
            pool.wait_ge(s["iota_ready"], 1)
            pool.wait_ge(chunk_done, ADA)
            pool.iota(IOTA[:, :], [[1, P]], 0, 0, allow_small_or_imprecise_dtypes=True).then_inc(s["iota_ready"], 1)
            pool.wait_ge(s["iota_ready"], 2)
            with pool.Fori(0, T // 16) as it:
                for q in range(2):
                    pool.wait_ge(s["oi_ready"], at(q + 1, 2, it))
                    pool.tensor_tensor(OI[:, q, :, :], OI[:, q, :, :],
                                       SLT[:, 2, bass.ds(it * 16 + 8 * q, 8)].unsqueeze(2).to_broadcast([P, 8, P]),
                                       ALU.mult).then_inc(s["gi_ready"], 1)
            pool.wait_ge(chunk_done, C0["up1"])
            pool.dma_start(HX[:, :, T:2 * T], a["ctxT"]).then_inc(s["ctx_landed"], 16)
            pool.dma_start(IDENT2[:, :], a["ident"]).then_inc(s["tables_landed"], 16)
            pool.wait_ge(s["norm_out"], 3 * KB)
            pool.dma_start(DIST[:, :, :, :], a["dist"]).then_inc(s["tables_landed"], 16)
            pool.wait_ge(chunk_done, C0["heads"])
            pool.dma_start(MASK[:, :, :, :], a["mask"]).then_inc(s["tables_landed"], 16)
            pool.dma_start(ROPE[:, :, :], a["rope"]).then_inc(s["tables_landed"], 16)
            pool.wait_ge(s["yr_ready"], RH)
            pool.dma_start(DFTL[:, :, :], a["dftl"]).then_inc(s["tables_landed"], 16)
            pool.dma_start(DFTD[:, :, :, :], a["dftd"]).then_inc(s["tables_landed"], 16)

        @block.scalar
        def _(act):
            step = Tally(act, s["act_step"])

            def split_hi(c, it=None, n=0):
                slot = c % 4
                act.wait_ge(landed[slot], at(16 * (c // 4 + 1), 4 * n, it))
                if c >= 4:
                    act.wait_ge(chunk_done, at(c - 3, n, it))
                act.activation(WH[:, slot, :], RAW[:, slot, :], ACT.Copy).then_inc(hi_ready, 1)

            def norm(n, src, tmp, width, rms, xh, ready, shift=None):
                for k in range(KB):
                    act.wait_ge(ready[0], ready[1](k))
                    act.activation(tmp[:, k, 0:width], src[:, k, 0:width], ACT.Square).then_inc(s["norm_sq"], 1)
                act.wait_ge(s["norm_sum"], n + 1)
                act.activation(rms[:, 0:width], ps[:, NORM_BANK[n], 0:width], ACT.Sqrt, bias=EPSC[:, 0:1],
                               scale=1.0 / D).then_inc(s["norm_rms"], 1)
                if xh is None:
                    return
                for k in range(KB):
                    act.wait_ge(s["norm_out"], n * KB + k + 1)
                    if shift is None:
                        ins = act.activation(xh[:, k, :], tmp[:, k, 0:width], ACT.Copy)
                    else:
                        for half in range(width // T):
                            cols = slice(half * T, half * T + T)
                            ins = act.activation(xh[:, k, cols], tmp[:, k, cols], ACT.Identity,
                                                 bias=shift(k, half))
                    ins.then_inc(s["norm_hi"], 1)

            act.wait_ge(s["x_landed"], 16)
            act.wait_ge(s["pool_consts"], 4)
            norm(0, H, TMP8, T, RMS, XH, (s["x_landed"], lambda k: 16))
            split_hi(0)
            split_hi(1)
            for c in range(0, 13):
                split_hi(c + 2)
                if c in (4, 8, 12):
                    n = c // 4 - 1
                    act.wait_ge(chunk_done, c + 1)
                    act.activation((KT, VT, SV)[n][:, :, :], ps[:, 4 + 2 * (n % 2):6 + 2 * (n % 2), :],
                                   (ACT.Copy, ACT.Copy, ACT.Gelu_apprx_tanh)[n]).then_inc(s["tok_ready"], 1)
            def glu(round_):
                if round_ == 0:
                    act.wait_ge(s["z_ready"], 1)
                    step.link(act.activation(LG1[:, :, :], ps[:, 4:6, :], ACT.Abs))
                    step.link(act.activation(LG1[:, :, :], LG1[:, :, :], ACT.Exp, scale=-1.0))
                    act.activation(LG1[:, :, :], LG1[:, :, :], ACT.Ln, bias=ONES[:, 0:1]).then_inc(s["ln_ready"], 1)
                elif round_ == 1:
                    act.wait_ge(s["sgu_var"], 1)
                    act.activation(MV[:, :, 1:2], MV[:, :, 1:2], ACT.Sqrt, bias=EPSC[:, 0:1]).then_inc(s["sgu_std"], 1)
                elif round_ == 2:
                    act.wait_ge(s["suffix_ready"], 1)
                    act.activation(EXS[:, :, :], ps[:, 6:8, :], ACT.Exp).then_inc(s["exs_ready"], 1)
                    act.activation(DEC[:, :, :], ps[:, 4, 0:16].rearrange("p (h c) -> p h c", h=HEADS),
                                   ACT.Exp).then_inc(s["exs_ready"], 1)
                elif round_ == 4:
                    act.wait_ge(s["o_ready"], 1)
                    o_ps = ps[:, 4:6, :].rearrange("p b (h t) -> p (b h) t", t=T)
                    act.activation(OG[:, :, :], o_ps, ACT.Copy, scale=float(P) ** -0.5).then_inc(s["og_ready"], 1)
                    act.activation(SQ2[:, :, :], o_ps, ACT.Square, scale=float(P) ** -0.5).then_inc(s["og_sq"], 1)
                elif round_ == 5:
                    act.wait_ge(s["og_sum"], 1)
                    act.activation(RMS2[:, :, :], ps[:, 6:8, :].rearrange("p b (h t) -> p (b h) t", t=T), ACT.Sqrt,
                                   bias=EPSC[:, 0:1], scale=1.0 / P).then_inc(s["og_rms"], 1)

            for n, func in enumerate((ACT.Copy, ACT.Silu, ACT.Gelu_apprx_tanh) + 4 * (ACT.Sigmoid,)):
                for j in range(4):
                    c = C0["feat"] + 4 * n + j
                    split_hi(c + 2)
                    act.wait_ge(chunk_done, c + 1)
                    act.activation(PROJ[:, 4 * n + j, :], ps[:, (U_FEAT + j) % 4, 0:T], func).then_inc(ring_evac, 1)
                    if j == 0:
                        glu(n)
                    if n == 6 and j == 2:
                        act.wait_ge(s["ya_ready"], 1)
                        act.activation(MH[:, 0:4, :], OG[:, :, :], ACT.Copy).then_inc(s["y_hi"], 1)
            act.wait_ge(s["yb_ready"], 1)
            act.activation(MH[:, 4:8, :], PROJ[:, 8:12, :], ACT.Copy).then_inc(s["y_hi"], 1)
            for m in range(KB):
                split_hi(C0["branch"] + m + 2)
                act.wait_ge(s["mg_ready"], m + 1)
                act.activation(XH[:, m, :], MG[:, m, :], ACT.Copy).then_inc(s["m_hi"], 1)
            with act.Fori(0, 2) as it:
                for j in range(4):
                    split_hi(C0["wout"] + j + 2, it, 4)
            norm(1, H, TMP8, T, RMS, XH, (ring_evac, lambda k: U_WOUT + k + 1))

            def query(c, j, it):
                act.wait_ge(chunk_done, at(c + 1, 4, it))
                act.wait_ge(s["scores_ready"], at(j + 1, 4, it))
                act.activation(QT[:, j, :], ps[:, (U_WQ + j) % 4, 0:T], ACT.Copy).then_inc(ring_evac, 1)

            def scores(i, j, it):
                act.wait_ge(s["scores_ready"], at(j + 5, 4, it) if it is not None else i + 5)
                dst = SC[:, bass.ds(it * 4 + j, 1), :, :] if it is not None else SC[:, i:i + 1, :, :]
                act.activation(dst, ps[:, 4 + j, 0:2 * P].rearrange("p (o a k) -> p o a k", o=1, a=TT),
                               ACT.Copy).then_inc(s["sc_ready"], 1)

            act.sem_inc(s["sc_ready"], 4)
            with act.Fori(0, 3) as it:
                for j in range(4):
                    split_hi(C0["wq"] + j + 2, it, 4)
                    query(C0["wq"] + j, j, it)
                    if j:
                        scores(None, j - 1, it)
                scores(None, 3, it)
            for j in range(4):
                c = C0["wq"] + 12 + j
                if c + 2 < ADA:
                    split_hi(c + 2)
                act.wait_ge(chunk_done, c + 1)
                act.wait_ge(s["scores_ready"], 13 + j)
                act.activation(QT[:, j, :], ps[:, (U_WQ + j) % 4, 0:T], ACT.Copy).then_inc(ring_evac, 1)
                if j:
                    scores(11 + j, j - 1, None)
            scores(15, 3, None)
            act.wait_ge(s["const_landed"], 16 * 11)
            act.activation(ID2[:, :], IDENT[0:2, 0:2], ACT.Copy).then_inc(s["id2_ready"], 1)
            act.activation(CS[:, :, :], CS[:, :, :], ACT.Silu).then_inc(s["cs_ready"], 1)
            step.link(act.activation(LGD[:, 1, :], LGD[:, 0, :], ACT.Abs))
            step.link(act.activation(LGD[:, 1, :], LGD[:, 1, :], ACT.Exp, scale=-1.0))
            act.activation(LGD[:, 2, :], LGD[:, 1, :], ACT.Ln, bias=ONES[:, 0:1]).then_inc(s["lgd_ready"], 1)
            act.sem_inc(s["mrow_ready"], 2)
            def mod_rows(g, it=None):
                act.wait_ge(chunk_done, at(ADA + 4 * g + 4, 8, it))
                dst = MROW[0:2, g * 512:g * 512 + 512] if it is None else MROW[0:2, bass.ds(it * 1024 + 512 * g, 512)]
                act.activation(dst, ps[0:2, 6 + g % 2, :], ACT.Copy).then_inc(s["mrow_ready"], 1)

            with act.Fori(0, 3) as it:
                for q in range(2):
                    mod_rows(q, it)
            act.wait_ge(s["vals_ready"], 1)
            act.activation(VAL[:, :, :, :], VAL[:, :, :, :], ACT.Exp).then_inc(s["val_exp"], 1)
            for g in range(6, ADA1):
                mod_rows(g)
            act.wait_ge(s["slots_turned"], 1)
            act.activation(SLT[:, 0:2, :], ps[:, 4, :].rearrange("p (a t) -> p a t", t=T), ACT.Copy)
            act.activation(SLT[:, 2, :], ps[:, 5, 0:T], ACT.Copy).then_inc(s["slots_ready"], 1)
            act.sem_inc(s["g_ready"], 2)
            with act.Fori(0, ADA2) as it:
                for u in range(4):
                    act.wait_ge(s["onehot_used"], at(u + 3, 4, it))
                    act.activation(G[:, :, bass.ds(it * 32 + 8 * u, 8)],
                                   ps[:, 2 * (u % 2):2 * (u % 2) + 2, :].rearrange("p b (t i) -> p i (b t)", t=4),
                                   ACT.Copy).then_inc(s["g_ready"], 1)
                act.wait_ge(chunk_done, at(ADA + 4 * ADA1 + 4, 4, it))
                act.activation(MROW2[0:2, bass.ds(it * 512, 512)], ps[0:2, 6, :], ACT.Copy).then_inc(s["mrow_ready"], 1)

            PC = C0["peer"]

            def expert_hi(e, it=None):
                act.wait_ge(s["gated_ready"], at(e + 1, 4, it))
                if it is not None or e >= 2:
                    act.wait_ge(chunk_done, at(PC + 3 + 2 * (e - 2) + 1, 8, it))
                src = G[:, e, :] if it is None else G[:, bass.ds(it * 4 + e, 1), :]
                dst = AH[:, e % 2, :] if it is None else AH[:, e % 2, :].unsqueeze(1)
                act.activation(dst, src, ACT.Copy).then_inc(s["a_hi"], 1)

            for c in range(4):
                split_hi(PC + c)
            act.wait_ge(chunk_done, PC + 1)
            act.activation(ps[:, 0, 0:T], ps[:, 0, 0:T], ACT.Gelu_apprx_tanh).then_inc(s["gelu_ready"], 1)
            expert_hi(0)

            def pair(e, it=None):
                split_hi(PC + 4 + 2 * e, it, 8)
                act.wait_ge(chunk_done, at(PC + (2 * e if e else 1) + 1, 8, it))
                act.activation(ps[:, (e + 1) % 4, 0:T], ps[:, (e + 1) % 4, 0:T],
                               ACT.Gelu_apprx_tanh).then_inc(s["gelu_ready"], 1)
                split_hi(PC + 5 + 2 * e, it, 8)
                expert_hi(e + 1, it)

            for e in range(2):
                pair(e)
            with act.Fori(0, 31) as it:
                for e in range(2, 6):
                    pair(e, it)
            split_hi(PC + 256)
            act.wait_ge(chunk_done, PC + 2 * 126 + 1)
            act.activation(ps[:, 127 % 4, 0:T], ps[:, 127 % 4, 0:T],
                           ACT.Gelu_apprx_tanh).then_inc(s["gelu_ready"], 1)
            expert_hi(127)
            split_hi(PC + 257)

            norm(2, H, TMP16, T, RMS5, None, (s["peer_added"], lambda k: k // 2 + 1))

            def ffn(n, up, down, width):
                with act.Fori(0, FF // 2) as it:
                    for f in range(2):
                        c = up + 2 * f
                        split_hi(c + 2, it, 4)
                        split_hi(c + 3, it, 4)
                        act.wait_ge(chunk_done, at(c + 1, 4, it))
                        act.activation(TA[:, f, 0:width], ps[:, 2 * f, 0:width],
                                       ACT.Silu).then_inc(s["ffn_silu"], 1)
                        act.wait_ge(s["ffn_prod"], at(n * FF + f + 3, 2, it))
                        act.activation(HIDH[:, bass.ds(it * 2 + f, 1), 0:width], HT[:, f, 0:width].unsqueeze(1),
                                       ACT.Copy).then_inc(s["ffn_hi"], 1)
                with act.Fori(0, 5) as it:
                    for j in range(4):
                        split_hi(down + j + 2, it, 4)
                for c in range(down + 22, min(down + 24, NCH)):
                    split_hi(c)

            act.wait_ge(s["ctx_landed"], 16)
            norm(3, HX, TMP16, 2 * T, RMS5, XH2_16, (s["norm_out"], lambda k: 2 * KB + k + 1),
                 lambda k, half: MOD[:, k, half:half + 1])
            ffn(0, C0["up1"], C0["down1"], 2 * T)
            norm(4, HX, TMP16, 2 * T, RMS5, XH2_16, (s["hx_ready"], lambda k: k + 1),
                 lambda k, half: MOD[:, 24 + k, half:half + 1])

            HC = C0["heads"]
            act.wait_ge(s["tables_landed"], 64)
            act.sem_inc(s["sg_ready"], 1)
            with act.Fori(0, RH) as it:
                act.wait_ge(s["p_ready"], it + 1)
                act.activation(EF[:, :, :], DIST[:, 0, :, :], ACT.Exp, scale=LGD[:, 3, bass.ds(it, 1)]).then_inc(s["decay_exp"], 1)
                act.activation(EB[:, :, :], DIST[:, 1, :, :], ACT.Exp, scale=LGD[:, 3, bass.ds(it + RH, 1)]).then_inc(s["decay_exp"], 1)
                for j in range(4):
                    split_hi(HC + j + 2, it, 12)
                act.wait_ge(chunk_done, at(HC + 4, 12, it))
                act.wait_ge(s["pv_ready"], it + 1)
                act.wait_ge(s["qk_ready"], at(1, 1, it))
                act.activation(KR[:, :, T:2 * T], ps[:, 2:4, T:2 * T], ACT.Copy).then_inc(s["kctx_ready"], 1)
                for j in range(4, 8):
                    split_hi(HC + j + 2, it, 12)
                act.wait_ge(chunk_done, at(HC + 8, 12, it))
                act.activation(VR[:, :, :], ps[:, 4:8, :], ACT.Copy).then_inc(s["v_ready"], 1)
                for j in range(8, 12):
                    split_hi(HC + j + 2, it, 12)
                act.wait_ge(chunk_done, at(HC + 12, 12, it))
                act.wait_ge(s["yt_ready"], it + 1)
                act.activation(SG[:, :, :], ps[:, 2:4, :].rearrange("p b (g t) -> p (b g) t", t=T),
                               ACT.Silu).then_inc(s["sg_ready"], 1)
                act.wait_ge(s["o_var"], at(1, 1, it))
                act.activation(OMV[:, :, 1:2], OMV[:, :, 1:2], ACT.Sqrt, bias=EPSC[:, 0:1]).then_inc(s["o_std"], 1)
                act.wait_ge(s["yt_ready"], at(2, 1, it))
                act.activation(YRH[:, bass.ds(it * 4, 4), :], YT[:, :, :], ACT.Copy).then_inc(s["yr_hi"], 1)
            for c in range(8):
                split_hi(C0["four"] + c + 2)
                if c in (3, 7):
                    n = c // 4
                    act.wait_ge(chunk_done, C0["four"] + c + 1)
                    if n == 0:
                        act.wait_ge(s["yr_ready"], RH)
                    act.activation(FT[:, :, n * 512:n * 512 + 512], ps[:, 4 + 2 * n:6 + 2 * n, :],
                                   ACT.Copy).then_inc(s["ft_ready"], 1)
            with act.Fori(0, 4) as it:
                for j in range(4):
                    split_hi(C0["gates"] + j + 2, it, 4)
                    act.wait_ge(chunk_done, at(C0["gates"] + j + 1, 4, it))
                    act.activation(GS[:, bass.ds(it * 4 + j, 1), :], ps[:, (U_GATES + j) % 4, 0:T].unsqueeze(1),
                                   ACT.Sigmoid).then_inc(ring_evac, 1)
            for n in range(KB):
                act.wait_ge(s["dft_tok"], n + 1)
                act.activation(AB[:, n, :], ps[:, 4 + n % 4, :], ACT.Copy).then_inc(s["ab_ready"], 1)
            act.wait_ge(s["dft_feat"], 1)
            act.activation(YFH[:, :, :], ps[:, 4:8, :].rearrange("p b (g t) -> p (b g) t", t=T),
                           ACT.Copy).then_inc(s["yf_hi"], 1)
            with act.Fori(0, 2) as it:
                for j in range(4):
                    for i in range(3):
                        split_hi(C0["proj"] + 3 * j + i + 2, it, 12)
                    act.wait_ge(s["mg2_ready"], at(j + 1, 4, it))
                    act.activation(XH2_8[:, bass.ds(it * 4 + j, 1), :], MG2[:, bass.ds(it * 4 + j, 1), :],
                                   ACT.Copy).then_inc(s["m2_hi"], 1)
            with act.Fori(0, 2) as it:
                for j in range(4):
                    split_hi(C0["wout2"] + j + 2, it, 4)
            norm(5, HX, TMP16, T, RMS5, XH2_8, (ring_evac, lambda k: U_WOUT2 + k + 1),
                 lambda k, half: MOD[:, 48 + k, half:half + 1])
            ffn(1, C0["up2"], C0["down2"], T)
            norm(6, HX, TMP16, T, RMS5, None, (s["hx_ready"], lambda k: KB + k + 1))

        @block.vector
        def _(dve):
            step = Tally(dve, s["dve_step"], s["dve_spacer"])

            def split_lo(c, it=None, n=0):
                slot = c % 4
                dve.wait_ge(hi_ready, at(split_index(c) + 1, n, it))
                dve.tensor_tensor(WL[:, slot, :], RAW[:, slot, :], WH[:, slot, :].bitcast(F32),
                                  ALU.subtract).then_inc(lo_ready, 1)

            def norm(n, src, tmp, width, rms, xh, xl, gain, shift=None, dst=None):
                dve.wait_ge(s["norm_rms"], n + 1)
                step.link(dve.reciprocal(rms[:, 0:width], rms[:, 0:width]))
                halves = [(h, slice(h * T, h * T + T)) for h in range(width // T)]

                def rest(k):
                    dve.wait_ge(s["norm_hi"], SPLIT_NORM[n] * KB + k + 1)
                    if shift is None:
                        ins = dve.tensor_tensor(xl[:, k, :], tmp[:, k, 0:width], xh[:, k, :].bitcast(F32), ALU.subtract)
                    else:
                        for half, cols in halves:
                            ins = dve.scalar_tensor_tensor(xl[:, k, cols], tmp[:, k, cols], shift(k, half),
                                                           xh[:, k, cols].bitcast(F32), ALU.add, ALU.subtract)
                    ins.then_inc(s["norm_lo"], 1)

                for k in range(KB):
                    for half, cols in halves:
                        ins = dve.scalar_tensor_tensor((tmp if dst is None else dst)[:, k, cols], src[:, k, cols],
                                                       gain(k, half), rms[:, cols], ALU.mult, ALU.mult)
                    ins.then_inc(s["norm_out"], 1)
                    if dst is None and k:
                        rest(k - 1)
                if dst is None:
                    rest(KB - 1)

            dve.wait_ge(s["cols_landed"], 16)
            norm(0, H, TMP8, T, RMS, XH, XL, lambda k, half: col("norm1", k))
            split_lo(0)
            split_lo(1)
            for c in range(0, 13):
                split_lo(c + 2)
                if c == 0:
                    dve.wait_ge(s["pool_consts"], 5)
                    dve.wait_ge(chunk_done, 1)
                    dve.tensor_copy(ALR[0:16, :], ps[0:16, 3, 0:T]).then_inc(ring_evac, U_FEAT)
            def glu(round_, j):
                if (round_, j) == (0, 1):
                    dve.wait_ge(s["tok_ready"], 3)
                    for tt in range(TT):
                        ins = dve.bn_stats(ST6[:, tt, :], SV[:, tt, :])
                    step.link(ins)
                    for tt in range(TT):
                        ins = dve.bn_aggr(MV[:, tt, :], ST6[:, tt, :])
                    ins.then_inc(s["sgu_var"], 1)
                elif (round_, j) == (0, 3):
                    dve.wait_ge(s["ln_ready"], 1)
                    dve.scalar_tensor_tensor(LOGA[:, :, :], ps[:, 4:6, :], 0.0, LG1[:, :, :], ALU.min,
                                             ALU.subtract).then_inc(s["loga_ready"], 1)
                elif (round_, j) == (1, 1):
                    dve.wait_ge(s["sgu_std"], 1)
                    step.link(dve.reciprocal(MV[:, :, 1:2], MV[:, :, 1:2]))
                    for tt in range(TT):
                        ins = dve.tensor_scalar(SV[:, tt, :], SV[:, tt, :], MV[:, tt, 0:1], MV[:, tt, 1:2],
                                                ALU.subtract, ALU.mult)
                    step.link(ins)
                elif (round_, j) == (1, 2):
                    dve.wait_ge(s["const_landed"], 16 * 11)
                    for tt in range(TT):
                        ins = dve.tensor_tensor(SV[:, tt, :], SV[:, tt, :], LNG[:, :], ALU.mult)
                    step.link(ins)
                elif (round_, j) == (1, 3):
                    for tt in range(TT):
                        ins = dve.tensor_tensor(SV[:, tt, :], SV[:, tt, :], LNB[:, :], ALU.add)
                    ins.then_inc(s["vn_ready"], 1)
                elif (round_, j) == (2, 1):
                    dve.wait_ge(s["exs_ready"], 1)
                    dve.tensor_tensor(KT[:, :, :], KT[:, :, :], EXS[:, :, :], ALU.mult).then_inc(s["kdec_ready"], 1)
                elif round_ == 3 and j < 3:
                    if j == 0:
                        dve.wait_ge(s["kv_ready"], 1)
                        dve.wait_ge(s["exs_ready"], 2)
                        step.link(dve.tensor_copy(ST[:, 0, :], ps[:, 4, :]))
                    c = j + 1
                    for h in range(HEADS):
                        hs = slice(h * P, h * P + P)
                        ins = dve.scalar_tensor_tensor(ST[:, c, hs], ST[:, c - 1, hs], DEC[:, h, c:c + 1],
                                                       ps[:, 4 + c, hs], ALU.mult, ALU.add)
                    if c < NCK - 1:
                        step.link(ins)
                    else:
                        ins.then_inc(s["state_ready"], 1)
                elif (round_, j) in ((5, 1), (5, 2), (5, 3), (6, 0)):
                    h = 4 * (round_ - 5) + j - 1
                    dve.wait_ge(s["og_rms"], 1)
                    dve.wait_ge(s["og_ready"], 1)
                    dve.wait_ge(ring_evac, U_FEAT + 8)
                    step.link(dve.reciprocal(RMS2[:, h, :], RMS2[:, h, :]))
                    step.link(dve.tensor_tensor(OG[:, h, :], OG[:, h, :], RMS2[:, h, :], ALU.mult))
                    step.link(dve.scalar_tensor_tensor(OG[:, h, :], OG[:, h, :], col("gla", h), PROJ[:, 4 + h, :],
                                                       ALU.mult, ALU.mult))
                    if h == HEADS - 1:
                        dve.sem_inc(s["ya_ready"], 1)
                elif (round_, j) == (6, 1):
                    dve.wait_ge(s["mixed_ready"], 1)
                    dve.wait_ge(ring_evac, U_FEAT + 12)
                    dve.tensor_tensor(PROJ[:, 8:12, :], PROJ[:, 8:12, :],
                                      ps[:, 4:6, :].rearrange("p b (g t) -> p (b g) t", t=T),
                                      ALU.mult).then_inc(s["yb_ready"], 1)

            for n in range(7):
                for j in range(4):
                    split_lo(C0["feat"] + 4 * n + j + 2)
                    glu(n, j)
            dve.wait_ge(s["y_hi"], 1)
            dve.tensor_tensor(ML[:, 0:4, :], OG[:, :, :], MH[:, 0:4, :].bitcast(F32), ALU.subtract).then_inc(s["y_lo"], 1)
            dve.wait_ge(s["yb_ready"], 1)
            dve.wait_ge(s["y_hi"], 2)
            dve.tensor_tensor(ML[:, 4:8, :], PROJ[:, 8:12, :], MH[:, 4:8, :].bitcast(F32),
                              ALU.subtract).then_inc(s["y_lo"], 1)
            gates = PROJ[:, 12:28, :].rearrange("p (b m) t -> p b m t", b=2)

            def merged_lo(m):
                dve.wait_ge(s["m_hi"], m + 1)
                dve.tensor_tensor(XL[:, m, :], MG[:, m, :], XH[:, m, :].bitcast(F32),
                                  ALU.subtract).then_inc(s["m_lo"], 1)

            for m in range(KB):
                split_lo(C0["branch"] + m + 2)
                if m:
                    merged_lo(m - 1)
                dve.wait_ge(chunk_done, C0["branch"] + m + 1)
                dve.tensor_tensor(TMPM[:, :, :], ps[:, (U_BRANCH + m) % 4, :].rearrange("p (b t) -> p b t", b=2),
                                  gates[:, :, m, :], ALU.mult).then_inc(ring_evac, 1)
                dve.wait_ge(ring_evac, U_BRANCH + m + 1)
                dve.tensor_tensor(MG[:, m, :], TMPM[:, 0, :], TMPM[:, 1, :], ALU.add).then_inc(s["mg_ready"], 1)
                dve.wait_ge(s["mg_ready"], m + 1)
            merged_lo(KB - 1)
            with dve.Fori(0, 2) as it:
                for j in range(4):
                    split_lo(C0["wout"] + j + 2, it, 4)
                    dve.wait_ge(chunk_done, at(C0["wout"] + j + 1, 4, it))
                    m = bass.ds(it * 4 + j, 1)
                    dve.tensor_tensor(H[:, m, :], ps[:, (U_WOUT + j) % 4, 0:T].unsqueeze(1), H[:, m, :],
                                      ALU.add).then_inc(ring_evac, 1)
            norm(1, H, TMP8, T, RMS, XH, XL, lambda k, half: col("norm2", k))
            def top_head(hd):
                dve.wait_ge(s["sc_ready"], hd * 2 + 6)
                step.link(dve.tensor_copy(STG[:, :, :, :], SC[:, bass.ds(hd * 2, 2), :, :]))
                units = [(side, tt) for side in range(2) for tt in range(TT)]
                step.apart()
                for sd, tt in units:
                    ins = dve.max(V16[:, sd, tt, 0:8], STG[:, sd, tt, :])
                step.link(ins)
                step.apart()
                for sd, tt in units:
                    dve.max_index(I16[:, sd, tt, 0:8], V16[:, sd, tt, 0:8], STG[:, sd, tt, :])
                    ins = dve.match_replace(STG2[:, sd, tt, :], V16[:, sd, tt, 0:8], STG[:, sd, tt, :], NEG)
                step.link(ins)
                step.apart()
                for sd, tt in units:
                    ins = dve.max(V16[:, sd, tt, 8:16], STG2[:, sd, tt, :])
                step.link(ins)
                step.apart()
                for sd, tt in units:
                    ins = dve.max_index(I16[:, sd, tt, 8:16], V16[:, sd, tt, 8:16], STG2[:, sd, tt, :])
                for tt in range(TT):
                    ins = dve.tensor_tensor(CAND[:, tt, :, :],
                                            V16[:, 0, tt, :].unsqueeze(2).to_broadcast([P, TOPK, TOPK]),
                                            V16[:, 1, tt, :].unsqueeze(1).to_broadcast([P, TOPK, TOPK]), ALU.add)
                step.link(ins)
                flat = [CAND[:, tt, :, :].rearrange("p a b -> p (a b)") for tt in range(TT)]
                flat2 = [CAND2[:, tt, :, :].rearrange("p a b -> p (a b)") for tt in range(TT)]
                h = bass.ds(hd, 1)
                step.link(dve.tensor_copy(IF[:, :, :, h, :].rearrange("p s t o k -> p (s t) o k"),
                                          I16[:, :, :, :].rearrange("p s t (o k) -> p (s t) o k", o=1)))
                step.apart()
                for tt in range(TT):
                    ins = dve.max(CV[:, tt, 0:8], flat[tt])
                step.link(ins)
                step.apart()
                for tt in range(TT):
                    dve.max_index(CI[:, tt, 0:8], CV[:, tt, 0:8], flat[tt])
                    ins = dve.match_replace(flat2[tt], CV[:, tt, 0:8], flat[tt], NEG)
                step.link(ins)
                step.apart()
                for tt in range(TT):
                    ins = dve.max(CV[:, tt, 8:16], flat2[tt])
                step.link(ins)
                step.apart()
                for tt in range(TT):
                    ins = dve.max_index(CI[:, tt, 8:16], CV[:, tt, 8:16], flat2[tt])
                step.link(ins)
                dve.tensor_copy(VAL[:, :, h, :], CV[:, :, :].unsqueeze(2))
                step.link(dve.tensor_copy(CIU[:, :, h, :], CI[:, :, :].unsqueeze(2)))

            with dve.Fori(0, 3) as it:
                step.begin(it, 11)
                for j in range(4):
                    split_lo(C0["wq"] + j + 2, it, 4)
                top_head(it)
                step.end(3)
            split_lo(ADA - 2)
            split_lo(ADA - 1)
            with dve.Fori(0, PEER_HEADS - 3) as it:
                step.begin(it, 11)
                top_head(it + 3)
                step.end(PEER_HEADS - 3)
            full = [P, PEER_HEADS, TOPK]
            big = [P, PEER_HEADS, TOPK, TOPK]
            for tt in range(TT):
                ins = dve.tensor_copy(GSUM[:, tt, :].unsqueeze(2), VAL[:, tt, :, 0:1])
            step.link(ins)
            for tt in range(TT):
                ins = dve.tensor_tensor(VAL[:, tt, :, :], VAL[:, tt, :, :],
                                        GSUM[:, tt, :].unsqueeze(2).to_broadcast(full), ALU.subtract)
            ins.then_inc(s["vals_ready"], 1)
            dve.tensor_scalar(IAU[:, 0, :, :, :], CIU[:, :, :, :], 4, None, ALU.logical_shift_right)
            step.link(dve.tensor_scalar(IAU[:, 1, :, :, :], CIU[:, :, :, :], 15, None, ALU.bitwise_and))
            step.link(dve.tensor_copy(IAF[:, :, :, :, :], IAU[:, :, :, :, :]))
            dve.wait_ge(s["iota_ready"], 1)
            for sd in range(2):
                for tt in range(TT):
                    step.link(dve.tensor_tensor(EQ[:, :, :, :], IAF[:, sd, tt, :, :].unsqueeze(3).to_broadcast(big),
                                                IOTA16[:, :].unsqueeze(1).unsqueeze(1).to_broadcast(big), ALU.is_equal))
                    step.link(dve.tensor_tensor(EQ[:, :, :, :], EQ[:, :, :, :],
                                                IF[:, sd, tt, :, :].unsqueeze(2).to_broadcast(big), ALU.mult))
                    step.link(dve.tensor_reduce(SEL[:, sd, tt, :, :], EQ[:, :, :, :], AXX, ALU.add))
            dve.wait_ge(s["val_exp"], 1)
            step.link(dve.tensor_reduce(GSUM[:, :, :], VAL[:, :, :, :], AXX, ALU.add))
            step.link(dve.reciprocal(GSUM[:, :, :], GSUM[:, :, :]))
            for tt in range(TT):
                ins = dve.tensor_tensor(SEL[:, 2, tt, :, :], VAL[:, tt, :, :],
                                        GSUM[:, tt, :].unsqueeze(2).to_broadcast(full), ALU.mult)
            ins.then_inc(s["sel_ready"], 1)
            dve.wait_ge(s["lgd_ready"], 1)
            dve.scalar_tensor_tensor(LGD[:, 3, :], LGD[:, 0, :], 0.0, LGD[:, 2, :], ALU.min,
                                     ALU.subtract).then_inc(s["lgd_done"], 1)
            dve.wait_ge(s["slots_ready"], 1)
            dve.wait_ge(s["iota_ready"], 2)
            wide = [P, 8, P]
            with dve.Fori(0, T // 16) as it:
                for q in range(2):
                    tok = bass.ds(it * 16 + 8 * q, 8)
                    dve.wait_ge(s["onehot_used"], at(q + 1, 2, it))
                    dve.tensor_tensor(OI[:, q, :, :], IOTA[:, :].unsqueeze(1).to_broadcast(wide),
                                      SLT[:, 0, tok].unsqueeze(2).to_broadcast(wide),
                                      ALU.is_equal).then_inc(s["oi_ready"], 1)
                    dve.tensor_tensor(OJ[:, q, :, :], IOTA[:, :].unsqueeze(1).to_broadcast(wide),
                                      SLT[:, 1, tok].unsqueeze(2).to_broadcast(wide),
                                      ALU.is_equal).then_inc(s["oj_ready"], 1)
            dve.wait_ge(s["mod_turned"], 1)
            bada = CL[:, COLS["bada"]:COLS["bada"] + MODB].unsqueeze(2).to_broadcast([P, MODB, 2])
            step.link(dve.tensor_tensor(MOD[:, :, :], ps[:, 7, 0:2 * MODB].rearrange("p (m c) -> p m c", c=2),
                                        bada, ALU.add))
            dve.sem_inc(s["mod_ready"], 1)
            for n, name in enumerate(("ffn1", "mix", "ffn2")):
                sc = MOD[:, 24 * n + 8:24 * n + 16, :]
                dve.scalar_tensor_tensor(SCG[:, n, :, :], sc, 1.0,
                                         CL[:, COLS[name]:COLS[name] + KB].unsqueeze(2).to_broadcast([P, KB, 2]),
                                         ALU.add, ALU.mult)
            dve.tensor_scalar(GH[:, 0, :, :], MOD[:, 16:24, :], 0.5, None, ALU.mult)
            step.link(dve.tensor_scalar(GH[:, 1, :, :], MOD[:, 64:72, :], 0.5, None, ALU.mult))

            PC = C0["peer"]

            def expert(e, it=None):
                q = e % 4
                dve.wait_ge(s["gelu_ready"], at(e + 1, 4, it))
                g = G[:, e:e + 1, :] if it is None else G[:, bass.ds(it * 4 + e, 1), :]
                dve.tensor_tensor(g, ps[:, q, 0:T].unsqueeze(1), g, ALU.mult).then_inc(s["gated_ready"], 1)

            def expert_lo(e, it=None):
                g = G[:, e:e + 1, :] if it is None else G[:, bass.ds(it * 4 + e, 1), :]
                dve.wait_ge(s["a_hi"], at(e + 1, 4, it))
                dve.tensor_tensor(AL[:, e % 2:e % 2 + 1, :], g, AH[:, e % 2:e % 2 + 1, :].bitcast(F32),
                                  ALU.subtract).then_inc(s["a_lo"], 1)

            for c in range(4):
                split_lo(PC + c)
            dve.wait_ge(s["g_ready"], T // 8 + 2)
            expert(0)
            expert_lo(0)

            def pair(e, it=None):
                split_lo(PC + 4 + 2 * e, it, 8)
                expert(e + 1, it)
                split_lo(PC + 5 + 2 * e, it, 8)
                expert_lo(e + 1, it)

            for e in range(2):
                pair(e)
            with dve.Fori(0, 31) as it:
                for e in range(2, 6):
                    pair(e, it)
            split_lo(PC + 256)
            expert(127)
            expert_lo(127)
            split_lo(PC + 257)
            dve.wait_ge(chunk_done, C0["up1"])
            for b in range(4):
                hb = H[:, 2 * b:2 * b + 2, :]
                dve.tensor_tensor(hb, hb, ps[:, 4 + b, :].rearrange("p (g t) -> p g t", t=T),
                                  ALU.add).then_inc(s["peer_added"], 1)
            norm(2, H, None, T, RMS5, None, None, lambda k, half: col("final", k), dst=HX)

            def ffn(n, up, down, width, halves):
                with dve.Fori(0, FF // 2) as it:
                    for f in range(2):
                        c = up + 2 * f
                        split_lo(c + 2, it, 4)
                        split_lo(c + 3, it, 4)
                        dve.wait_ge(chunk_done, at(c + 2, 4, it))
                        dve.wait_ge(s["ffn_silu"], at(n * FF + f + 1, 2, it))
                        dve.tensor_tensor(HT[:, f, 0:width], TA[:, f, 0:width], ps[:, 2 * f + 1, 0:width],
                                          ALU.mult).then_inc(s["ffn_prod"], 1)
                        dve.wait_ge(s["ffn_hi"], at(n * FF + f + 1, 2, it))
                        dve.tensor_tensor(HIDL[:, bass.ds(it * 2 + f, 1), 0:width], HT[:, f, 0:width].unsqueeze(1),
                                          HIDH[:, bass.ds(it * 2 + f, 1), 0:width].bitcast(F32),
                                          ALU.subtract).then_inc(s["ffn_lo"], 1)
                with dve.Fori(0, 5) as it:
                    for j in range(4):
                        split_lo(down + j + 2, it, 4)
                for c in range(down + 22, min(down + 24, NCH)):
                    split_lo(c)
                dve.wait_ge(chunk_done, down + FF)
                for m in range(KB):
                    for half in range(halves):
                        src = ps[:, m, half * T:half * T + T] if width > T else ps[:, 4 + m // 2, (m % 2) * T:(m % 2) * T + T]
                        dst = HX[:, m, half * T:half * T + T]
                        ins = dve.scalar_tensor_tensor(dst, src, GH[:, n, m, half:half + 1], dst, ALU.mult, ALU.add)
                    ins.then_inc(s["hx_ready"], 1)

            dve.wait_ge(s["ctx_landed"], 16)
            dve.sem_inc(s["ffn_prod"], 2)
            norm(3, HX, TMP16, 2 * T, RMS5, XH2_16, XL2_16,
                 lambda k, half: SCG[:, 0, k, half:half + 1], lambda k, half: MOD[:, k, half:half + 1])
            ffn(0, C0["up1"], C0["down1"], 2 * T, 2)
            norm(4, HX, TMP16, 2 * T, RMS5, XH2_16, XL2_16,
                 lambda k, half: SCG[:, 1, k, half:half + 1], lambda k, half: MOD[:, 24 + k, half:half + 1])

            HC = C0["heads"]
            dve.wait_ge(s["tables_landed"], 64)
            for name in ("p_ready", "on_ready", "yt_ready"):
                dve.sem_inc(s[name], 1)
            with dve.Fori(0, RH) as it:
                step.begin(it, 7)
                dve.wait_ge(s["decay_exp"], at(2, 2, it))
                dve.tensor_tensor(EF[:, 0:2, :], EF[:, 0:2, :], MASK[:, 0, :, :], ALU.mult)
                step.link(dve.tensor_tensor(EB[:, 0:2, :], EB[:, 0:2, :], MASK[:, 1, :, :], ALU.mult))
                step.link(dve.tensor_tensor(EF[:, :, :], EF[:, :, :], EB[:, :, :], ALU.add))
                for j in range(4):
                    split_lo(HC + j + 2, it, 12)
                dve.wait_ge(chunk_done, at(HC + 4, 12, it))
                cos, sin = ROPE[:, 0, :], ROPE[:, 1, :]
                for b, dst in ((0, QR), (2, KR)):
                    dve.tensor_tensor(RT[:, 0, :], ps[:, b, 0:T], cos, ALU.mult)
                    dve.tensor_tensor(RT[:, 1, :], ps[:, b + 1, 0:T], sin, ALU.mult)
                    dve.tensor_tensor(RT[:, 2, :], ps[:, b, 0:T], sin, ALU.mult)
                    step.link(dve.tensor_tensor(RT[:, 3, :], ps[:, b + 1, 0:T], cos, ALU.mult))
                    dve.tensor_tensor(dst[:, 0, 0:T], RT[:, 0, :], RT[:, 1, :], ALU.subtract)
                    ins = dve.tensor_tensor(dst[:, 1, 0:T], RT[:, 2, :], RT[:, 3, :], ALU.add)
                    if b == 0:
                        step.link(ins)
                ins.then_inc(s["qk_ready"], 1)
                for j in range(4, 8):
                    split_lo(HC + j + 2, it, 12)
                for j in range(8, 10):
                    split_lo(HC + j + 2, it, 12)
                dve.wait_ge(s["s_ready"], at(1, 1, it))
                dve.scalar_tensor_tensor(PT[:, :, :], ps[:, 0:2, :].rearrange("p b (g t) -> p (b g) t", t=T),
                                         1.0 / 16.0, EF[:, :, :], ALU.mult, ALU.mult).then_inc(s["p_ready"], 1)
                for j in range(10, 12):
                    split_lo(HC + j + 2, it, 12)
                dve.wait_ge(s["pv_ready"], at(2, 1, it))
                for tt in range(TT):
                    ins = dve.bn_stats(OST6[:, tt, :], ps[:, 4 + tt, :])
                step.link(ins)
                step.apart()
                for tt in range(TT):
                    ins = dve.bn_aggr(OMV[:, tt, :], OST6[:, tt, :])
                ins.then_inc(s["o_var"], 1)
                dve.wait_ge(s["o_std"], at(1, 1, it))
                step.link(dve.reciprocal(OMV[:, :, 1:2], OMV[:, :, 1:2]))
                for tt in range(TT):
                    ins = dve.tensor_scalar(ON[:, tt, :], ps[:, 4 + tt, :], OMV[:, tt, 0:1], OMV[:, tt, 1:2],
                                            ALU.subtract, ALU.mult)
                ins.then_inc(s["on_ready"], 1)
                dve.wait_ge(s["on_turned"], at(1, 1, it))
                dve.wait_ge(s["sg_ready"], at(2, 1, it))
                for v in range(4):
                    gain = CL[:, bass.ds(it * 4 + (COLS["gn"] + v), 1)]
                    ins = dve.scalar_tensor_tensor(YT[:, v, :], ps[:, 6 + v // 2, (v % 2) * T:(v % 2) * T + T],
                                                   gain, SG[:, v, :], ALU.mult, ALU.mult)
                ins.then_inc(s["yt_ready"], 1)
                dve.wait_ge(s["yr_hi"], at(1, 1, it))
                dve.tensor_tensor(YRL[:, bass.ds(it * 4, 4), :], YT[:, :, :],
                                  YRH[:, bass.ds(it * 4, 4), :].bitcast(F32), ALU.subtract).then_inc(s["yr_ready"], 1)
                step.end(RH)
            for c in range(8):
                split_lo(C0["four"] + c + 2)
            with dve.Fori(0, 4) as it:
                for j in range(4):
                    split_lo(C0["gates"] + j + 2, it, 4)
            dve.wait_ge(s["yf_hi"], 1)
            dve.tensor_tensor(YFL[:, :, :], ps[:, 4:8, :].rearrange("p b (g t) -> p (b g) t", t=T),
                              YFH[:, :, :].bitcast(F32), ALU.subtract).then_inc(s["yf_ready"], 1)
            with dve.Fori(0, 2) as it:
                for j in range(4):
                    for i in range(3):
                        split_lo(C0["proj"] + 3 * j + i + 2, it, 12)
                    dve.wait_ge(chunk_done, at(C0["proj"] + 3 * j + 3, 12, it))
                    gates = GS[:, :, :].rearrange("p (b m) t -> p b m t", b=2)[:, :, bass.ds(it * 4 + j, 1), :]
                    dve.tensor_tensor(TMP2[:, :, :].unsqueeze(2),
                                      ps[:, (U_PROJ + j) % 4, :].rearrange("p (b o t) -> p b o t", b=2, o=1),
                                      gates, ALU.mult).then_inc(ring_evac, 1)
                    dve.wait_ge(ring_evac, at(U_PROJ + j + 1, 4, it))
                    m = bass.ds(it * 4 + j, 1)
                    dve.tensor_tensor(MG2[:, m, :], TMP2[:, 0:1, :], TMP2[:, 1:2, :],
                                      ALU.add).then_inc(s["mg2_ready"], 1)
                    dve.wait_ge(s["m2_hi"], at(j + 1, 4, it))
                    dve.tensor_tensor(XL2_8[:, m, :], MG2[:, m, :], XH2_8[:, m, :].bitcast(F32),
                                      ALU.subtract).then_inc(s["m2_lo"], 1)
            with dve.Fori(0, 2) as it:
                for j in range(4):
                    split_lo(C0["wout2"] + j + 2, it, 4)
                    dve.wait_ge(chunk_done, at(C0["wout2"] + j + 1, 4, it))
                    m = bass.ds(it * 4 + j, 1)
                    dve.scalar_tensor_tensor(HX[:, m, 0:T], ps[:, (U_WOUT2 + j) % 4, 0:T].unsqueeze(1),
                                             MOD[:, bass.ds(it * 4 + (40 + j), 1), 0], HX[:, m, 0:T],
                                             ALU.mult, ALU.add).then_inc(ring_evac, 1)
            norm(5, HX, TMP16, T, RMS5, XH2_8, XL2_8,
                 lambda k, half: SCG[:, 2, k, half:half + 1], lambda k, half: MOD[:, 48 + k, half:half + 1])
            ffn(1, C0["up2"], C0["down2"], T, 1)
            norm(6, HX, None, T, RMS5, None, None, lambda k, half: col("last", k), dst=HX)

        @block.tensor
        def _(pe):
            def split_ready(c, it=None, n=0):
                pe.wait_ge(lo_ready, at(split_index(c) + 1, n, it))

            def bank_free(u, it=None, n=4):
                if u >= 4:
                    pe.wait_ge(ring_evac, at(u - 3, n, it))

            def product(dst, wh, wl, xh, xl, start, stop, check=True):
                pe.matmul(dst, wh, xh, start=start, stop=False, skip_group_check=not check)
                pe.matmul(dst, wh, xl, start=False, stop=False, skip_group_check=not check)
                return pe.matmul(dst, wl, xh, start=False, stop=stop, skip_group_check=not check)

            def feature_chunk(c, dst, xh, xl, it=None, n=0, k0=0, start=True, stop=True, norm=None, parts=None):
                split_ready(c, it, n)
                slot = c % 4
                for k in range(KB):
                    if norm is not None:
                        pe.wait_ge(s["norm_lo"], SPLIT_NORM[norm] * KB + k + 1)
                    if parts is not None:
                        pe.wait_ge(parts, k + 1)
                    w = slice(k * P, k * P + P)
                    ins = product(dst, WH[:, slot, w], WL[:, slot, w], xh[:, k0 + k, :], xl[:, k0 + k, :],
                                  start and k == 0, stop and k == KB - 1)
                ins.then_inc(chunk_done, 1)

            def token_chunk(c, part, bank, tiles, xh, xl, it=None, n=0):
                split_ready(c, it, n)
                slot = c % 4
                for kk in range(2):
                    k = 2 * part + kk
                    w = slice(kk * 512, kk * 512 + 512)
                    for tt in range(tiles):
                        t = slice(tt * P, tt * P + P)
                        dst = ps[:, bank + tt, :]
                        pe.matmul(dst, xh[:, k, t], WH[:, slot, w], start=(k == 0), stop=False)
                        pe.matmul(dst, xl[:, k, t], WH[:, slot, w], start=False, stop=False)
                        ins = pe.matmul(dst, xh[:, k, t], WL[:, slot, w], start=False, stop=(k == KB - 1))
                ins.then_inc(chunk_done, 1)

            def norm_sum(n, tmp, width):
                for k in range(KB):
                    pe.wait_ge(s["norm_sq"], n * KB + k + 1)
                    ins = pe.matmul(ps[:, NORM_BANK[n], 0:width], ONES[:, :], tmp[:, k, 0:width], start=(k == 0), stop=(k == KB - 1))
                ins.then_inc(s["norm_sum"], 1)

            pe.wait_ge(s["pool_consts"], 4)
            norm_sum(0, TMP8, T)
            feature_chunk(0, ps[:, 3, 0:T], XH, XL, norm=0)
            for c in range(1, 13):
                n, part = divmod(c - 1, 4)
                if n == 2 and part == 0:
                    pe.wait_ge(s["tok_ready"], 1)
                token_chunk(c, part, 4 + 2 * (n % 2), TT, XH, XL)
            pe.wait_ge(ring_evac, U_FEAT)

            def glu(round_):
                if round_ == 0:
                    pe.wait_ge(s["const_landed"], 16 * 11)
                    pe.wait_ge(s["tok_ready"], 3)
                    for tt in range(TT):
                        ins = pe.matmul(ps[:, 4 + tt, :], ALR[0:17, tt * P:tt * P + P], WA2[:, :], start=True, stop=True)
                    ins.then_inc(s["z_ready"], 1)
                elif round_ == 2:
                    pe.wait_ge(s["loga_ready"], 1)
                    for tt in range(TT):
                        pe.matmul(ps[:, 6 + tt, :], UM[:, :], LOGA[:, tt, :], start=True, stop=True)
                    for tt in range(TT):
                        for h in range(HEADS):
                            ins = pe.matmul(ps[:, 4, h * NCK + 2 * tt:h * NCK + 2 * tt + 2],
                                            LOGA[:, tt, h * P:h * P + P], BONES[:, :], start=True, stop=True)
                    ins.then_inc(s["suffix_ready"], 1)
                elif round_ == 3:
                    pe.wait_ge(s["kdec_ready"], 1)
                    pe.wait_ge(s["exs_ready"], 2)
                    for c in range(NCK):
                        rows = slice((c % 2) * CHUNK, (c % 2) * CHUNK + CHUNK)
                        for h in range(HEADS):
                            hs = slice(h * P, h * P + P)
                            ins = pe.matmul(ps[:, 4 + c, hs], KT[rows, c // 2, hs], VT[rows, c // 2, hs],
                                            start=True, stop=True)
                    ins.then_inc(s["kv_ready"], 1)
                elif round_ == 4:
                    pe.wait_ge(s["state_ready"], 1)
                    for h in range(HEADS):
                        for c in range(NCK):
                            t0 = (h % 2) * T + c * CHUNK
                            ins = pe.matmul(ps[:, 4 + h // 2, t0:t0 + CHUNK], ST[:, c, h * P:h * P + P],
                                            PROJ[:, h, c * CHUNK:c * CHUNK + CHUNK], start=True, stop=True)
                    ins.then_inc(s["o_ready"], 1)
                elif round_ == 5:
                    pe.wait_ge(s["og_sq"], 1)
                    for b in range(2):
                        ins = pe.matmul(ps[:, 6 + b, :], ONES[:, :], SQ2[:, 2 * b:2 * b + 2, :], start=True, stop=True)
                    ins.then_inc(s["og_sum"], 1)
                elif round_ == 6:
                    pe.wait_ge(s["vn_ready"], 1)
                    pe.wait_ge(s["og_ready"], 1)
                    pe.wait_ge(s["pool_consts"], 5)
                    for g in range(4):
                        for nb in range(TT):
                            t0 = (g % 2) * T + nb * P
                            dst = ps[:, 4 + g // 2, t0:t0 + P]
                            pe.matmul(dst, SV[:, nb, g * P:g * P + P], WST[:, g, :], start=True, stop=False)
                            ins = pe.matmul(dst, ONES[0:1, :], BS[0:1, g * P:g * P + P], start=False, stop=True)
                    ins.then_inc(s["mixed_ready"], 1)

            for n in range(7):
                glu(n)
                for j in range(4):
                    bank_free(U_FEAT + 4 * n + j)
                    feature_chunk(C0["feat"] + 4 * n + j, ps[:, (U_FEAT + j) % 4, 0:T], XH, XL)
            for j in range(KB):
                c = C0["branch"] + j
                bank_free(U_BRANCH + j)
                split_ready(c)
                for k in range(KB):
                    if j == 0 and k % 4 == 0:
                        pe.wait_ge(s["y_lo"], k // 4 + 1)
                    w = slice(k * P, k * P + P)
                    dst = ps[:, (U_BRANCH + j) % 4, (k // 4) * T:(k // 4) * T + T]
                    ins = product(dst, WH[:, c % 4, w], WL[:, c % 4, w], MH[:, k, :], ML[:, k, :],
                                  k % 4 == 0, k % 4 == 3)
                ins.then_inc(chunk_done, 1)
            with pe.Fori(0, 2) as it:
                for j in range(4):
                    bank_free(U_WOUT + j, it)
                    feature_chunk(C0["wout"] + j, ps[:, (U_WOUT + j) % 4, 0:T], XH, XL, it, 4,
                                  parts=None if j else s["m_lo"])
            norm_sum(1, TMP8, T)
            def scores(j, it):
                pe.wait_ge(ring_evac, at(U_WQ + j + 1, 4, it))
                pe.wait_ge(s["sc_ready"], at(j + 1, 4, it))
                for tt in range(TT):
                    ins = pe.matmul(ps[:, 4 + j, tt * P:tt * P + P], QT[:, j, tt * P:tt * P + P], K12T[:, j % 2, :],
                                    start=True, stop=True)
                ins.then_inc(s["scores_ready"], 1)

            pe.sem_inc(s["scores_ready"], 4)
            with pe.Fori(0, 4) as it:
                for j in range(4):
                    bank_free(U_WQ + j, it)
                    feature_chunk(C0["wq"] + j, ps[:, (U_WQ + j) % 4, 0:T], XH, XL, it, 4, norm=None if j else 1)
                    if j:
                        scores(j - 1, it)
                scores(3, it)
            pe.wait_ge(s["cs_ready"], 1)
            pe.wait_ge(s["sc_ready"], 16 + 4)
            def mod_chunk(c, j, bank, it=None, n=0):
                pe.wait_ge(landed[c % 4], at(16 * (c // 4 + 1), 4 * n, it))
                for kk in range(2):
                    k = 2 * j + kk
                    ins = pe.matmul(ps[0:2, bank, :], CS[:, k, :], RAW[:, c % 4, kk * 512:kk * 512 + 512],
                                    start=(k == 0), stop=(k == KB - 1))
                ins.then_inc(chunk_done, 1)

            def turn_rows(rows, m0, count):
                for i in range(count):
                    m = m0 + i
                    ins = pe.transpose(ps[:, 7, 2 * m:2 * m + 2], rows[0:2, i * P:i * P + P], ID2[:, :])
                return ins

            with pe.Fori(0, ADA1 // 2) as it:
                for q in range(2):
                    pe.wait_ge(s["mrow_ready"], at(q + 1, 2, it))
                    for j in range(4):
                        mod_chunk(ADA + 4 * q + j, j, 6 + q, it, 8)
            pe.wait_ge(s["id2_ready"], 1)
            pe.wait_ge(s["mrow_ready"], ADA1 + 2)
            turn_rows(MROW, 0, 4 * ADA1)
            pe.wait_ge(s["sel_ready"], 1)
            for n in range(3):
                for tt in range(TT):
                    ins = pe.transpose(ps[:, 4 + n // 2, (n % 2) * T + tt * P:(n % 2) * T + tt * P + P],
                                       SEL[:, n, tt, :, :].rearrange("p h k -> p (h k)"), IDENT[:, :])
            ins.then_inc(s["slots_turned"], 1)
            pe.sem_inc(s["onehot_used"], 2)
            with pe.Fori(0, ADA2) as it:
                for u in range(4):
                    q = u % 2
                    pe.wait_ge(s["oj_ready"], at(u + 1, 4, it))
                    pe.wait_ge(s["gi_ready"], at(u + 1, 4, it))
                    pe.wait_ge(s["g_ready"], at(u + 1, 4, it))
                    for t in range(8):
                        ins = pe.matmul(ps[:, 2 * q + t // 4, (t % 4) * P:(t % 4) * P + P], OJ[:, q, t, :],
                                        OI[:, q, t, :], start=True, stop=True)
                    ins.then_inc(s["onehot_used"], 1)
                    if u == 0:
                        pe.wait_ge(s["mrow_ready"], at(ADA1 + 2, 1, it))
                    mod_chunk(ADA + 4 * ADA1 + u, u, 6, it, 4)
            pe.wait_ge(s["mrow_ready"], MODB // 4 + 2)
            turn_rows(MROW2, 4 * ADA1, 4 * ADA2).then_inc(s["mod_turned"], 1)

            PC = C0["peer"]

            def up(e, c, it=None):
                feature_chunk(c, ps[:, e % 4, 0:T], XH, XL, it, 8)

            def down(e, c, it=None, last=False):
                split_ready(c, it, 8)
                pe.wait_ge(s["a_lo"], at(e + 1, 4, it))
                for m in range(KB):
                    w = slice(m * P, m * P + P)
                    ins = product(ps[:, 4 + m // 2, (m % 2) * T:(m % 2) * T + T], WH[:, c % 4, w], WL[:, c % 4, w],
                                  AH[:, e % 2, :], AL[:, e % 2, :], False, last, check=False)
                ins.then_inc(chunk_done, 1)

            pe.wait_ge(s["g_ready"], T // 8 + 2)
            up(0, PC)
            up(1, PC + 1)
            pe.wait_ge(s["mod_ready"], 1)
            for b in range(4):
                for i in range(4):
                    pe.matmul(ps[:, 4 + b, i * P:i * P + P], ZR[0:1, :], ONES[0:1, :], start=(i == 0), stop=False,
                              skip_group_check=True)

            def pair(e, it=None):
                if e >= 2:
                    pe.wait_ge(s["gated_ready"], at(e - 1, 4, it))
                up(e + 2, PC + 2 + 2 * e, it)
                down(e, PC + 3 + 2 * e, it)

            for e in range(2):
                pair(e)
            with pe.Fori(0, 31) as it:
                for e in range(2, 6):
                    pair(e, it)
            down(126, PC + 254)
            down(127, PC + 255, last=True)
            norm_sum(2, TMP16, T)

            def ffn(n, upc, downc, width, xh, xl):
                with pe.Fori(0, FF // 2) as it:
                    for j in range(4):
                        pe.wait_ge(s["ffn_prod"], at(n * FF + j // 2 + 1, 2, it))
                        feature_chunk(upc + j, ps[:, j, 0:width], xh, xl, it, 4, norm=None if j else (3, 5)[n])
                pe.wait_ge(s["ffn_lo"], FF * (n + 1))

                def hidden(c, k, it=None, step_=4, first=False, last=False):
                    split_ready(c, it, step_)
                    kk = slice(k, k + 1) if it is None else bass.ds(it * 4 + k, 1)
                    for m in range(KB):
                        w = slice(m * P, m * P + P)
                        if width > T:
                            dst, opens = ps[:, m, :].unsqueeze(1), True
                        else:
                            dst, opens = ps[:, 4 + m // 2, (m % 2) * T:(m % 2) * T + T].unsqueeze(1), m % 2 == 0
                        ins = product(dst, WH[:, c % 4, w], WL[:, c % 4, w], HIDH[:, kk, 0:width], HIDL[:, kk, 0:width],
                                      first and opens, last, check=False)
                    ins.then_inc(chunk_done, 1)

                hidden(downc, 0, first=True)
                with pe.Fori(0, 5) as it:
                    for j in range(4):
                        hidden(downc + 1 + j, 1 + j, it)
                hidden(downc + 21, 21, last=True)

            norm_sum(3, TMP16, 2 * T)
            ffn(0, C0["up1"], C0["down1"], 2 * T, XH2_16, XL2_16)
            norm_sum(4, TMP16, 2 * T)
            HC = C0["heads"]
            pe.sem_inc(s["pv_ready"], 1)
            with pe.Fori(0, RH) as it:
                pe.wait_ge(s["p_ready"], it + 1)
                pe.wait_ge(s["sg_ready"], it + 1)
                for j in range(2):
                    feature_chunk(HC + j, ps[:, j, 0:T], XH2_16[:, :, 0:T], XL2_16[:, :, 0:T], it, 12,
                                  norm=None if j else 4)
                for j in range(2, 4):
                    feature_chunk(HC + j, ps[:, j, :], XH2_16, XL2_16, it, 12)
                pe.wait_ge(s["on_ready"], it + 1)
                pe.wait_ge(s["yt_ready"], it + 1)
                for j in range(4):
                    token_chunk(HC + 4 + j, j, 4, 4, XH2_16, XL2_16, it, 12)
                pe.wait_ge(s["qk_ready"], at(1, 1, it))
                pe.wait_ge(s["kctx_ready"], at(1, 1, it))
                for jt in range(4):
                    for d in range(2):
                        ins = pe.matmul(ps[:, jt // 2, (jt % 2) * T:(jt % 2) * T + T], KR[:, d, jt * P:jt * P + P],
                                        QR[:, d, :], start=(d == 0), stop=(d == 1))
                ins.then_inc(s["s_ready"], 1)
                for j in range(4):
                    feature_chunk(HC + 8 + j, ps[:, 2 + j // 2, (j % 2) * T:(j % 2) * T + T],
                                  XH2_16[:, :, 0:T], XL2_16[:, :, 0:T], it, 12)
                pe.wait_ge(s["p_ready"], at(2, 1, it))
                pe.wait_ge(s["v_ready"], at(1, 1, it))
                for tt in range(TT):
                    for jt in range(4):
                        ins = pe.matmul(ps[:, 4 + tt, :], PT[:, jt, tt * P:tt * P + P], VR[:, jt, :],
                                        start=(jt == 0), stop=(jt == 3))
                ins.then_inc(s["pv_ready"], 1)
                pe.wait_ge(s["on_ready"], at(2, 1, it))
                for v in range(4):
                    for tt in range(TT):
                        t0 = (v % 2) * T + tt * P
                        ins = pe.transpose(ps[:, 6 + v // 2, t0:t0 + P], ON[:, tt, v * P:v * P + P], IDENT2[:, :])
                ins.then_inc(s["on_turned"], 1)
            pe.wait_ge(s["on_ready"], RH + 1)
            pe.wait_ge(s["yt_ready"], RH + 1)
            for c in range(8):
                token_chunk(C0["four"] + c, c % 4, 4 + 2 * (c // 4), TT, XH2_16, XL2_16)
            pe.wait_ge(s["sg_ready"], RH + 1)
            with pe.Fori(0, 4) as it:
                for j in range(4):
                    bank_free(U_GATES + j, it)
                    feature_chunk(C0["gates"] + j, ps[:, (U_GATES + j) % 4, 0:T], XH2_16[:, :, 0:T], XL2_16[:, :, 0:T], it, 4)
            pe.wait_ge(s["ft_ready"], 2)
            pe.wait_ge(s["tables_landed"], 96)
            for n in range(KB):
                if n >= 4:
                    pe.wait_ge(s["ab_ready"], n - 3)
                for tt in range(TT):
                    ins = pe.matmul(ps[:, 4 + n % 4, :], FT[:, tt, n * P:n * P + P], DFTL[:, tt, :],
                                    start=(tt == 0), stop=(tt == TT - 1))
                ins.then_inc(s["dft_tok"], 1)
            pe.wait_ge(s["ab_ready"], KB)
            for n in range(KB):
                dst = ps[:, 4 + n // 2, (n % 2) * T:(n % 2) * T + T]
                for cb in range(2):
                    for part in range(2):
                        ins = pe.matmul(dst, DFTD[:, cb, part, (n % 2) * P:(n % 2) * P + P],
                                        AB[:, 2 * (n // 2) + cb, part * T:part * T + T],
                                        start=(cb == 0 and part == 0), stop=(cb == 1 and part == 1))
            ins.then_inc(s["dft_feat"], 1)
            pe.wait_ge(s["yr_ready"], RH)
            with pe.Fori(0, 2) as it:
                for j in range(4):
                    c, b = C0["proj"] + 3 * j, (U_PROJ + j) % 4
                    bank_free(U_PROJ + j, it)
                    feature_chunk(c, ps[:, b, 0:T], YRH, YRL, it, 12, stop=False)
                    feature_chunk(c + 1, ps[:, b, 0:T], YRH, YRL, it, 12, k0=KB, start=False)
                    pe.wait_ge(s["yf_ready"], 1)
                    feature_chunk(c + 2, ps[:, b, T:2 * T], YFH, YFL, it, 12)
            with pe.Fori(0, 2) as it:
                for j in range(4):
                    bank_free(U_WOUT2 + j, it)
                    feature_chunk(C0["wout2"] + j, ps[:, (U_WOUT2 + j) % 4, 0:T], XH2_8, XL2_8, it, 4,
                                  parts=None if j else s["m2_lo"])
            norm_sum(5, TMP16, T)
            ffn(1, C0["up2"], C0["down2"], T, XH2_8, XL2_8)
            norm_sum(6, TMP16, T)


def lay_out(x):
    import numpy as np

    def features(w):
        k, n = w.shape
        return w.reshape(k // P, P, n // P, P).transpose(2, 1, 0, 3).reshape(n // P, P, -1)

    def tokens(w):
        return w.reshape(4, 2, P, 512).transpose(0, 2, 1, 3).reshape(4, P, 1024)

    def vec(v):
        return v.reshape(-1, P).T

    w = x["w_in"][0]
    q, k, v, r, alr, su, sv, ga, gb = np.split(w, [512, 1024, 1536, 2048, 2064, 2576, 3088, 4112], axis=1)
    parts = [features(np.concatenate([alr, np.zeros((D, P - 16), alr.dtype)], axis=1))]
    parts += [tokens(k), tokens(v), tokens(sv)]
    parts += [features(np.concatenate([q, r, su, ga, gb], axis=1))]
    parts += [features(np.concatenate([x["w_branch_a"][0], x["w_branch_b"][0]], axis=0)), features(x["w_out"][0])]
    parts += [features(x["peer_wq"][0])]
    parts += [tokens(x["w_ada_2"][0][:, n:n + 512]) for n in range(0, N_MOD * D, 512)]
    up = features(x["peer_u"][0].T)
    down = x["peer_v"][0].reshape(P, P, D)
    order = [up[0:1], up[1:2]]
    for e in range(P):
        if e + 2 < P:
            order.append(up[e + 2:e + 3])
        order.append(down[e:e + 1])
    parts += order

    def ffn(w13, w2):
        f = features(w13).reshape(2, FF, P, 1024).transpose(1, 0, 2, 3).reshape(2 * FF, P, 1024)
        return [f, w2.reshape(FF, P, D)]

    parts += ffn(x["w13_ffn1_2"][0], x["w2_ffn1_2"][0])
    w = x["w_in_2"][0]
    for h in range(RH):
        for c0 in (256 * h, 1024 + 256 * h):
            parts += [features(w[:, c0:c0 + 256:2]), features(w[:, c0 + 1:c0 + 256:2])]
        parts += [tokens(w[:, 2048 + 512 * h:2560 + 512 * h]), features(w[:, 4096 + 512 * h:4608 + 512 * h])]
    parts += [tokens(w[:, 6144:6656]), tokens(w[:, 6656:7168]), features(w[:, 7168:9216])]
    ret, four = features(x["p_ret_2"][0]), features(x["p_four_2"][0])
    for m in range(KB):
        parts += [ret[m:m + 1, :, 0:1024], ret[m:m + 1, :, 1024:2048], four[m:m + 1]]
    parts += [features(x["w_out_2"][0])]
    parts += ffn(x["w13_ffn2_2"][0], x["w2_ffn2_2"][0])
    stream = np.concatenate(parts, axis=0)
    assert stream.shape == (NCH, P, 1024)

    def acts(v):
        return v.T.reshape(KB, P, T).transpose(1, 0, 2)

    one = np.float64(1)
    i, p = np.arange(T)[None, None, :], np.arange(P)[:, None, None]
    j = p + P * np.arange(2)[None, :, None]
    fwd = np.concatenate([np.maximum(i - j, 0), T + i - j], axis=1)
    bwd = np.concatenate([np.maximum(j - i, 0), T - i + j], axis=1)
    inv = np.float32(10000.0) ** (-np.arange(64, dtype=np.float32) / np.float32(64))
    row, column = (np.arange(T) // 64).astype(np.float32), (np.arange(T) % 64).astype(np.float32)
    ang = np.concatenate([inv[:, None] * row[None], inv[:, None] * column[None]], axis=0).astype(np.float64)
    turn = 2 * np.pi * one / T
    lt = turn * ((np.arange(T)[:, None] * np.arange(T)[None, :]) % T)
    cos, sin = (np.cos(lt) / 16).reshape(2, P, T), (np.sin(lt) / 16).reshape(2, P, T)
    sidx = np.arange(P)
    same = sidx[:, None] // CHUNK == sidx[None, :] // CHUNK
    f = np.float32
    out = {
        "wstream": stream,
        "xT": acts(x["x"][0]), "ctxT": acts(x["ctx_2"][0]),
        "cols": np.concatenate([vec(x[n].reshape(-1)) for n in (
            "norm1_g", "norm2_g", "final_g", "gla_norm_g", "norm_ffn1_2", "norm_mix_2", "norm_ffn2_2",
            "norm_final_2", "ret_gn_w_2", "b_ada_2")], axis=1),
        "wa2b": np.concatenate([x["w_gate_up"][0], x["b_gate"]], axis=0),
        "wsT": x["sgu_w"][0].transpose(2, 0, 1), "bs": x["sgu_b"].reshape(1, 512),
        "lng": np.repeat(x["sgu_ln_g"], P, axis=0), "lnb": np.repeat(x["sgu_ln_b"], P, axis=0),
        "k12T": np.stack([x["peer_k1"][0].T, x["peer_k2"][0].T], axis=1),
        "cT": np.stack([vec(x["c_2"][0]), vec(x["c_ctx_2"])], axis=2),
        "decays": np.repeat(np.concatenate([x["decay_fwd_2"], x["decay_bwd_2"]], axis=1), P, axis=0),
        "umat": ((sidx[:, None] > sidx[None, :]) & same).astype(f) / f(TAU),
        "bones": (sidx[:, None] // CHUNK == np.arange(2)[None, :]).astype(f) / f(TAU),
        "ident": np.eye(P, dtype=f),
        "dist": np.stack([fwd, bwd], axis=1).astype(f),
        "mask": np.stack([i >= j, j >= i], axis=1).astype(f),
        "rope": np.stack([np.cos(ang), np.sin(ang)], axis=1).astype(f),
        "dftl": np.concatenate([cos, sin], axis=2).transpose(1, 0, 2).astype(f),
        "dftd": np.stack([cos, -sin], axis=2).transpose(1, 0, 2, 3).astype(f),
    }
    return {n: np.ascontiguousarray(v) for n, v in out.items()}


def kernel(**inputs):
    import numpy as _np
    import concourse.bacc as _bacc
    from concourse.bass_utils import run_bass_kernel_spmd as _run

    laid = lay_out({n: _np.asarray(v) for n, v in inputs.items()})
    nc = _bacc.Bacc("TRN2", target_bir_lowering=False, num_devices=1)
    arrays, args = {}, {}
    for n, v in laid.items():
        arrays[f"in_{n}"] = v
        args[n] = nc.dram_tensor(f"in_{n}", v.shape, mybir.dt.from_np(v.dtype), kind="ExternalInput").ap()
    out = nc.dram_tensor("out_0", (P, KB, T), F32, kind="ExternalOutput").ap()
    build(nc, args, out)
    r = _run(nc, [arrays], core_ids=[0])
    got = r.results[0]["out_0"]
    return got.transpose(2, 1, 0).reshape(1, T, D)
```
